# Optimizing a Trainium2 kernel written in Bass

```python
import math
import jax
import jax.numpy as jnp
from jax import lax
import numpy as np

D_MODEL = 1024
BATCH = 1
SEQ = 512
DEPTH = 2

GRID_W = 64
CTX_LEN = 256
NORM_EPS = 1e-6
HEAD_DIM = D_MODEL // 16

GLA_HEADS = 4
GLA_DV = HEAD_DIM
GLA_DK = HEAD_DIM // 2
GLA_GATE_RANK = 16
GLA_TAU = 16.0
GLA_CHUNK = 64

NAT_HEADS = 4
NAT_DH = HEAD_DIM
NAT_WIN_R = 8
NAT_WIN_C = 16

DIFF_HEADS = 4
DIFF_DH = HEAD_DIM
Q_BLOCK = 128
ROPE_BASE = 10000.0

PEER_HEADS = 8
PEER_NKEYS = 128
PEER_EXPERTS = PEER_NKEYS * PEER_NKEYS
PEER_QDIM = 128
PEER_HALF = PEER_QDIM // 2
PEER_TOPK = 16
PEER_TOKEN_BLOCK = 128

GLA_WIDTH = GLA_HEADS * GLA_DV
NAT_WIDTH = NAT_HEADS * NAT_DH
DIFF_WIDTH = DIFF_HEADS * 2 * DIFF_DH
MIX_WIDTH = GLA_WIDTH + NAT_WIDTH + DIFF_WIDTH
PROJ_SIZES = (GLA_HEADS * GLA_DK, GLA_HEADS * GLA_DK, GLA_WIDTH, GLA_WIDTH, GLA_GATE_RANK, GLA_GATE_RANK,
              NAT_WIDTH, NAT_WIDTH, NAT_WIDTH, DIFF_WIDTH, DIFF_WIDTH, DIFF_WIDTH)
PROJ_WIDTH = sum(PROJ_SIZES)

kernel_name = "hybrid_gla_natten_diffattn_peer_dit"

def rms_norm(x, g):
    xf = x.astype(jnp.float32)
    y = xf * lax.rsqrt(jnp.mean(xf * xf, axis=-1, keepdims=True) + NORM_EPS)
    return (y * g.astype(jnp.float32)).astype(x.dtype)

def modulate(x, g, shift, scale):
    return rms_norm(x, g) * (1 + scale) + shift

def heads(t, n):
    return t.reshape(t.shape[:-1] + (n, t.shape[-1] // n))

def flip(t):
    return jnp.flip(t, axis=1)

def split_proj(p):
    points = np.cumsum(PROJ_SIZES)[:-1].tolist()
    return jnp.split(p, points, axis=-1)

def head_rms(o, g):
    of = o.astype(jnp.float32)
    of = of * lax.rsqrt(jnp.mean(of * of, axis=-1, keepdims=True) + NORM_EPS)
    return of.reshape(of.shape[:-2] + (-1,)) * g.astype(jnp.float32)

def gla_scan(q, k, v, g, s0):
    B, L, H, K = q.shape
    V = v.shape[-1]
    n = L // GLA_CHUNK

    def to_chunks(t):
        return t.reshape(B, n, GLA_CHUNK, H, t.shape[-1]).transpose(1, 0, 3, 2, 4).astype(jnp.float32)

    qc, kc, vc, gc = (to_chunks(t) for t in (q, k, v, g))
    mask = jnp.tril(jnp.ones((GLA_CHUNK, GLA_CHUNK), dtype=bool))[:, :, None]

    def step(s, inp):
        qi, ki, vi, gi = inp
        b = jnp.cumsum(gi, axis=2)
        diff = b[:, :, :, None, :] - b[:, :, None, :, :]
        decay = jnp.exp(jnp.where(mask, diff, -jnp.inf))
        a = jnp.einsum('bhik,bhjk,bhijk->bhij', qi, ki, decay)
        o = jnp.einsum('bhij,bhjv->bhiv', a, vi) + jnp.einsum('bhik,bhkv->bhiv', qi * jnp.exp(b), s)
        b_last = b[:, :, -1, :]
        s_new = jnp.exp(b_last)[..., None] * s + jnp.einsum(
            'bhjk,bhjv->bhkv', ki * jnp.exp(b_last[:, :, None, :] - b), vi)
        return s_new, o

    s_fin, o = lax.scan(step, s0.astype(jnp.float32), (qc, kc, vc, gc))
    o = o.transpose(1, 0, 3, 2, 4).reshape(B, L, H, V)
    return o, s_fin

def gla_final_state(k, v, g):
    b = jnp.cumsum(g.astype(jnp.float32), axis=1)
    w = jnp.exp(b[:, -1:] - b)
    return jnp.einsum('blhk,blhv->bhkv', k.astype(jnp.float32) * w, v.astype(jnp.float32))

def gla_inputs(p, gate_up, gate_b):
    q = heads(p[0], GLA_HEADS) * GLA_DK ** -0.5
    k = heads(p[1], GLA_HEADS)
    v = heads(p[2], GLA_HEADS)
    g_f = heads(jax.nn.log_sigmoid((p[4] @ gate_up[0] + gate_b[0]).astype(jnp.float32)) / GLA_TAU, GLA_HEADS)
    g_b = heads(jax.nn.log_sigmoid((p[5] @ gate_up[1] + gate_b[1]).astype(jnp.float32)) / GLA_TAU, GLA_HEADS)
    return q, k, v, g_f, g_b

def gla_output(o, r, norm_g):
    return (head_rms(o, norm_g) * jax.nn.silu(r.astype(jnp.float32))).astype(r.dtype)

def gla_mix(p, pc, gate_up, gate_b, norm_g, need_ctx):
    q, k, v, g_f, g_b = gla_inputs(p, gate_up, gate_b)
    qc, kc, vc, gc_f, gc_b = gla_inputs(pc, gate_up, gate_b)
    s_f = gla_final_state(kc, vc, gc_f)
    s_b = gla_final_state(flip(kc), flip(vc), flip(gc_b))
    o = gla_scan(q, k, v, g_f, s_f)[0] + flip(gla_scan(flip(q), flip(k), flip(v), flip(g_b), s_b)[0])
    y = gla_output(o, p[3], norm_g)
    if not need_ctx:
        return y, None
    zero = jnp.zeros_like(s_f)
    oc = gla_scan(qc, kc, vc, gc_f, zero)[0] + flip(gla_scan(flip(qc), flip(kc), flip(vc), flip(gc_b), zero)[0])
    return y, gla_output(oc, pc[3], norm_g)

def neighbourhood_attention(q, k, v, kc, vc, rpb):
    B, S, H, d = q.shape
    rows = S // GRID_W
    wr = min(NAT_WIN_R, rows)
    r = jnp.arange(rows)
    row_start = jnp.clip(r - wr // 2, 0, rows - wr)
    row_idx = row_start[:, None] + jnp.arange(wr)[None, :]
    cidx = jnp.arange(GRID_W)
    col_start = jnp.clip(cidx - NAT_WIN_C // 2, 0, GRID_W - NAT_WIN_C)
    col_mask = (cidx[None, :] >= col_start[:, None]) & (cidx[None, :] < col_start[:, None] + NAT_WIN_C)
    dr = row_idx - r[:, None] + NAT_WIN_R - 1
    dc = jnp.clip(cidx[None, :] - cidx[:, None] + NAT_WIN_C - 1, 0, 2 * NAT_WIN_C - 2)
    bias = rpb[:, dr[:, None, :, None], dc[None, :, None, :]].astype(jnp.float32)

    scale = d ** -0.5
    qg = q.reshape(B, rows, GRID_W, H, d)
    kg = k.reshape(B, rows, GRID_W, H, d)[:, row_idx]
    vg = v.reshape(B, rows, GRID_W, H, d)[:, row_idx]
    s_win = jnp.einsum('brchd,brjkhd->bhrcjk', qg, kg).astype(jnp.float32) * scale + bias[None]
    s_win = jnp.where(col_mask[:, None, :], s_win, -jnp.inf)
    s_ctx = jnp.einsum('brchd,bmhd->bhrcm', qg, kc).astype(jnp.float32) * scale
    n_win = wr * GRID_W
    s = jnp.concatenate([s_win.reshape(B, H, rows, GRID_W, n_win), s_ctx], axis=-1)
    p = jax.nn.softmax(s, axis=-1).astype(v.dtype)
    p_win = p[..., :n_win].reshape(B, H, rows, GRID_W, wr, GRID_W)
    p_ctx = p[..., n_win:]
    o = jnp.einsum('bhrcjk,brjkhd->brchd', p_win, vg) + jnp.einsum('bhrcm,bmhd->brchd', p_ctx, vc)
    return o.reshape(B, S, H * d)

def softmax_attention(q, k, v):
    s = jnp.einsum('bqhd,bkhd->bhqk', q, k).astype(jnp.float32) * q.shape[-1] ** -0.5
    p = jax.nn.softmax(s, axis=-1).astype(v.dtype)
    return jnp.einsum('bhqk,bkhd->bqhd', p, v)

def rope_1d(x, pos):
    half = x.shape[-1] // 2
    inv = ROPE_BASE ** (-jnp.arange(half, dtype=jnp.float32) / half)
    ang = pos.astype(jnp.float32)[:, None] * inv[None, :]
    cos = jnp.cos(ang)[None, :, None, :]
    sin = jnp.sin(ang)[None, :, None, :]
    x1 = x[..., :half].astype(jnp.float32)
    x2 = x[..., half:].astype(jnp.float32)
    return jnp.concatenate([x1 * cos - x2 * sin, x2 * cos + x1 * sin], axis=-1).astype(x.dtype)

def rope_axial(x, row, col):
    h = x.shape[-1] // 2
    return jnp.concatenate([rope_1d(x[..., :h], row), rope_1d(x[..., h:], col)], axis=-1)

def diff_inputs(p):
    q = p[9].reshape(p[9].shape[:-1] + (DIFF_HEADS, 2, DIFF_DH))
    k = p[10].reshape(p[10].shape[:-1] + (DIFF_HEADS, 2, DIFF_DH))
    v = heads(p[11], DIFF_HEADS)
    return q[..., 0, :], q[..., 1, :], k[..., 0, :], k[..., 1, :], v

def diff_core(q1, q2, k1, k2, v, lam):
    scale = q1.shape[-1] ** -0.5
    a1 = jax.nn.softmax(jnp.einsum('bqhd,bkhd->bhqk', q1, k1).astype(jnp.float32) * scale, axis=-1)
    a2 = jax.nn.softmax(jnp.einsum('bqhd,bkhd->bhqk', q2, k2).astype(jnp.float32) * scale, axis=-1)
    return jnp.einsum('bhqk,bkhe->bqhe', (a1 - lam * a2).astype(v.dtype), v)

def diff_attention_latent(q1, q2, k1, k2, v, k1c, k2c, vc, lam):
    B, S, H, d = q1.shape
    k1a = jnp.concatenate([k1c, k1], axis=1)
    k2a = jnp.concatenate([k2c, k2], axis=1)
    va = jnp.concatenate([vc, v], axis=1)
    nb = S // Q_BLOCK

    def to_blocks(t):
        return jnp.swapaxes(t.reshape(B, nb, Q_BLOCK, H, d), 0, 1)

    def attend(qs):
        return diff_core(qs[0], qs[1], k1a, k2a, va, lam)

    o = lax.map(attend, (to_blocks(q1), to_blocks(q2)))
    return jnp.swapaxes(o, 0, 1).reshape(B, S, H, 2 * d)

def token_mix(h, hc, row, col, w_in, gate_up, gate_b, gla_g, rpb, lam_vec, diff_g, lam_init, need_ctx):
    p = split_proj(h @ w_in)
    pc = split_proj(hc @ w_in)
    y_gla, yc_gla = gla_mix(p, pc, gate_up, gate_b, gla_g, need_ctx)
    nq, nk, nv = (heads(t, NAT_HEADS) for t in p[6:9])
    nqc, nkc, nvc = (heads(t, NAT_HEADS) for t in pc[6:9])
    y_nat = neighbourhood_attention(nq, nk, nv, nkc, nvc, rpb)
    lv = lam_vec.astype(jnp.float32)
    lam = jnp.exp(jnp.sum(lv[0] * lv[1])) - jnp.exp(jnp.sum(lv[2] * lv[3])) + lam_init
    q1, q2, k1, k2, dv = diff_inputs(p)
    q1c, q2c, k1c, k2c, dvc = diff_inputs(pc)
    q1, q2, k1, k2 = (rope_axial(t, row, col) for t in (q1, q2, k1, k2))
    o_diff = diff_attention_latent(q1, q2, k1, k2, dv, k1c, k2c, dvc, lam)
    y_diff = head_rms(o_diff, diff_g) * (1.0 - lam_init)
    y = jnp.concatenate([y_gla, y_nat.astype(h.dtype), y_diff.astype(h.dtype)], axis=-1)
    if not need_ctx:
        return y, None
    yc_nat = softmax_attention(nqc, nkc, nvc).reshape(hc.shape[:-1] + (NAT_WIDTH,))
    yc_diff = head_rms(diff_core(q1c, q2c, k1c, k2c, dvc, lam), diff_g) * (1.0 - lam_init)
    yc = jnp.concatenate([yc_gla, yc_nat.astype(hc.dtype), yc_diff.astype(hc.dtype)], axis=-1)
    return y, yc

def peer_ffn(h, wq, subkeys, u, v):
    B, L, D = h.shape
    hb = h.reshape(-1, PEER_TOKEN_BLOCK, D)

    def block(hx):
        tb = hx.shape[0]
        q = (hx @ wq).reshape(tb, PEER_HEADS, 2, PEER_HALF)
        s1 = jnp.einsum('thd,nd->thn', q[:, :, 0], subkeys[0]).astype(jnp.float32)
        s2 = jnp.einsum('thd,nd->thn', q[:, :, 1], subkeys[1]).astype(jnp.float32)
        v1, i1 = lax.top_k(s1, PEER_TOPK)
        v2, i2 = lax.top_k(s2, PEER_TOPK)
        cand = (v1[..., :, None] + v2[..., None, :]).reshape(tb, PEER_HEADS, -1)
        cid = (i1[..., :, None] * PEER_NKEYS + i2[..., None, :]).reshape(tb, PEER_HEADS, -1)
        top, pos = lax.top_k(cand, PEER_TOPK)
        eid = jnp.take_along_axis(cid, pos, axis=-1)
        gate = jax.nn.softmax(top, axis=-1)
        act = jax.nn.gelu(jnp.einsum('td,thkd->thk', hx, u[eid]).astype(jnp.float32))
        return jnp.einsum('thk,thkd->td', (gate * act).astype(hx.dtype), v[eid])

    return lax.map(block, hb).reshape(B, L, D)

def setup_inputs(seed: int = 0) -> dict:
    key = jax.random.key(seed)
    ks = jax.random.split(key, 21)
    D = D_MODEL

    def nrm(k, shape, s):
        return jax.random.normal(k, shape, jnp.float32) * s

    return {
        "x": nrm(ks[0], (BATCH, SEQ, D), 1.0),
        "c": nrm(ks[1], (BATCH, D), 1.0),
        "ctx": nrm(ks[2], (BATCH, CTX_LEN, D), 1.0),
        "c_ctx": nrm(ks[3], (D,), 1.0),
        "ada_w": nrm(ks[4], (DEPTH, D, 6 * D), 0.5 * D ** -0.5),
        "ada_b": nrm(ks[5], (DEPTH, 6 * D), 0.01),
        "norm1_g": 1.0 + nrm(ks[6], (DEPTH, D), 0.02),
        "norm2_g": 1.0 + nrm(ks[7], (DEPTH, D), 0.02),
        "w_in": nrm(ks[8], (DEPTH, D, PROJ_WIDTH), D ** -0.5),
        "gla_gate_up": nrm(ks[9], (DEPTH, 2, GLA_GATE_RANK, GLA_HEADS * GLA_DK), GLA_GATE_RANK ** -0.5),
        "gla_gate_b": 1.0 + nrm(ks[10], (DEPTH, 2, GLA_HEADS * GLA_DK), 0.1),
        "gla_norm_g": 1.0 + nrm(ks[11], (DEPTH, GLA_WIDTH), 0.02),
        "nat_rpb": nrm(ks[12], (DEPTH, NAT_HEADS, 2 * NAT_WIN_R - 1, 2 * NAT_WIN_C - 1), 0.1),
        "diff_lambda": nrm(ks[13], (DEPTH, 4, DIFF_DH), 0.1),
        "diff_norm_g": 1.0 + nrm(ks[14], (DEPTH, DIFF_WIDTH), 0.02),
        "w_out": nrm(ks[15], (DEPTH, MIX_WIDTH, D), MIX_WIDTH ** -0.5),
        "peer_wq": nrm(ks[16], (DEPTH, D, PEER_HEADS * PEER_QDIM), D ** -0.5),
        "peer_subkeys": nrm(ks[17], (DEPTH, 2, PEER_NKEYS, PEER_HALF), PEER_HALF ** -0.5),
        "peer_u": nrm(ks[18], (DEPTH, PEER_EXPERTS, D), D ** -0.5),
        "peer_v": nrm(ks[19], (DEPTH, PEER_EXPERTS, D), PEER_HEADS ** -0.5),
        "final_g": 1.0 + nrm(ks[20], (D,), 0.02),
    }

def reference(x, c, ctx, c_ctx, ada_w, ada_b, norm1_g, norm2_g, w_in, gla_gate_up, gla_gate_b, gla_norm_g,
              nat_rpb, diff_lambda, diff_norm_g, w_out, peer_wq, peer_subkeys, peer_u, peer_v, final_g):
    B, S, D = x.shape
    t = jnp.arange(S)
    row = t // GRID_W
    col = t % GRID_W
    xc = ctx
    for l in range(DEPTH):
        last = l == DEPTH - 1
        lam_init = 0.8 - 0.6 * math.exp(-0.3 * l)
        mod = jnp.split((jax.nn.silu(c) @ ada_w[l] + ada_b[l])[:, None, :], 6, axis=-1)
        mod_c = jnp.split(jax.nn.silu(c_ctx) @ ada_w[l] + ada_b[l], 6, axis=-1)
        h = modulate(x, norm1_g[l], mod[0], mod[1])
        hc = modulate(xc, norm1_g[l], mod_c[0], mod_c[1])
        y, yc = token_mix(h, hc, row, col, w_in[l], gla_gate_up[l], gla_gate_b[l], gla_norm_g[l],
                          nat_rpb[l], diff_lambda[l], diff_norm_g[l], lam_init, not last)
        x = x + mod[2] * (y @ w_out[l])
        h2 = modulate(x, norm2_g[l], mod[3], mod[4])
        x = x + mod[5] * peer_ffn(h2, peer_wq[l], peer_subkeys[l], peer_u[l], peer_v[l])
        if not last:
            xc = xc + mod_c[2] * (yc @ w_out[l])
            hc2 = modulate(xc, norm2_g[l], mod_c[3], mod_c[4])
            xc = xc + mod_c[5] * peer_ffn(hc2, peer_wq[l], peer_subkeys[l], peer_u[l], peer_v[l])
    return rms_norm(x, final_g)


_drawn_inputs = setup_inputs


def setup_inputs(seed=0):
    import zlib

    import numpy as np

    out = dict(_drawn_inputs(seed))
    spreads = {}
    factors = {'ada_b': 3.184,
     'norm1_g': 5.821,
     'norm2_g': 15.387,
     'gla_gate_b': 5.074,
     'gla_norm_g': 8.0,
     'nat_rpb': 8.0,
     'diff_lambda': 5.866,
     'diff_norm_g': 37.867,
     'final_g': 8.747}
    for name, (base, spread) in spreads.items():
        noise = np.random.default_rng([zlib.crc32(name.encode()), seed]).standard_normal(out[name].shape)
        drawn = base * np.exp(spread * noise) if base else spread * noise
        out[name] = jnp.asarray(drawn.astype(out[name].dtype))
    for name, factor in factors.items():
        out[name] = (out[name] * factor).astype(out[name].dtype)
    return out
```

```python
from contextlib import ExitStack
from math import exp as _exp

import numpy as np

import concourse.bass as bass
from concourse import mybir

ALU = mybir.AluOpType
ACT = mybir.ActivationFunctionType
F32 = mybir.dt.float32
U8 = mybir.dt.uint8
U32 = mybir.dt.uint32
AX_X = mybir.AxisListType.X

P = 128
D = 1024
KD = D // P
DEPTH = 2
SEQ, CTX = 512, 256
CT, LT = CTX // P, SEQ // P
NT = CT + LT
TOK = NT * P
GRID_W = 64
EPS = 1e-6
GQ, GK, GV, GR, GG = 0, 128, 256, 512, 768
NQ, NK, NV = 800, 1056, 1312
DQ, DK, DV = 1568, 2080, 2592
PROJ = 3104
HEADS = 4
PROJ_CHUNKS = [(GQ, 512, True), (GR, 288, True), (NQ, 256, False), (NK, 512, True),
               (DQ, 512, False), (DK, 512, True), (DV, 512, True)]
LEVELS = [64, 32, 16, 8, 4, 2, 1]
NLEV = len(LEVELS) + 1
TAU = 16.0
PH, TOPK, NKEYS = 8, 16, 128
SLOTS = PH * TOPK
EXPERTS = NKEYS * NKEYS
RING = 8
NEG = -3.0e38


def lam_init(l):
    return 0.8 - 0.6 * _exp(-0.3 * l)


def shape_constants():
    t = np.arange(SEQ)
    inv = np.float32(10000.0) ** (-np.arange(16, dtype=np.float32) / np.float32(16))
    rope = np.zeros((SEQ, 2, 2, 2, 16), np.float32)
    for a, pos in enumerate((t // GRID_W, t % GRID_W)):
        ang = pos.astype(np.float32)[:, None] * inv[None, :].astype(np.float32)
        rope[:, 0, a, 0] = rope[:, 0, a, 1] = np.cos(ang)
        rope[:, 1, a, 0] = -np.sin(ang)
        rope[:, 1, a, 1] = np.sin(ang)
    j, i = np.arange(P)[:, None], np.arange(P)[None, :]
    levels = np.zeros((P, 2, NLEV, P), np.float32)
    for n, s in enumerate(LEVELS):
        same = j // (2 * s) == i // (2 * s)
        levels[:, 0, n] = same & (j // s % 2 == 0) & (i // s % 2 == 1)
        levels[:, 1, n] = same & (j // s % 2 == 1) & (i // s % 2 == 0)
    levels[:, :, NLEV - 1] = (i == j)[:, None]
    block = (np.arange(P)[:, None] // 32 == np.arange(256)[None, :] // 64).astype(np.float32)
    q, k = np.arange(P)[:, None] % GRID_W, np.arange(GRID_W)[None, :]
    start = np.clip(q - 8, 0, GRID_W - 16)
    window = np.where((k >= start) & (k < start + 16), 0.0, -1.0e30).astype(np.float32)
    iota = np.broadcast_to(np.arange(16, dtype=np.float32), (P, 16))
    return {
        "rope": rope.reshape(SEQ, 128), "levels": levels.reshape(P, 2 * NLEV * P),
        "small": np.concatenate([np.eye(P, dtype=np.float32), block, window, iota], axis=1),
    }


class Stage:

    def __init__(self, nc, name):
        self.nc, self.name, self.sems, self.gathers, self.stack = nc, name, [], [], ExitStack()

    def sem(self, name):
        s = self.stack.enter_context(self.nc.semaphore(f"{self.name}_{name}"))
        self.sems.append(s)
        return s

    def sb(self, name, shape, dt=F32):
        return self.stack.enter_context(self.nc.sbuf_tensor(f"{self.name}_{name}", shape, dt))

    def ps(self, name, shape):
        return self.stack.enter_context(self.nc.psum_tensor(f"{self.name}_{name}", shape, F32))

    def __enter__(self):
        return self

    def __exit__(self, *e):
        if e[0] is None:
            with self.nc.Block() as block:
                @block.sync
                def _(sp):
                    for s in self.sems:
                        sp.sem_clear(s)

                if self.gathers:
                    @block.gpsimd
                    def _(pool):
                        pool.dma_reset()
                        for s in self.gathers:
                            pool.sem_clear(s)
        self.stack.close()


def linker(eng, sem):
    count = [0]

    def link(ins):
        count[0] += 1
        ins.then_inc(sem, 1)
        eng.wait_ge(sem, count[0])
    return link


def load(eng, dst, src, sem):
    eng.dma_start(dst, src).then_inc(sem, 16)


def row_bcast(ap, n=P):
    return bass.AP(ap.tensor, ap.offset, [[0, n]] + [list(x) for x in ap.ap][-1:])


class Model:
    pass


def setup(nc, m):
    NC, RINGW = 12, 4
    with Stage(nc, "setup") as st:
        w = st.sb("ada", [P, RINGW, KD, 512])
        cond = st.sb("cond", [2 * KD, P])
        silu_rows = st.sb("silurows", [2 * KD, P])
        rows = st.sb("rows", [2, NC * 512])
        pad = st.sb("pad", [DEPTH * HEADS * 15, P])
        acc = st.ps("acc", [P, 4, 512])
        tr = st.ps("tr", [P, 512])
        consts, conds, biases, rpb = st.sem("consts"), st.sem("conds"), st.sem("biases"), st.sem("rpb")
        ada = [st.sem(f"ada{i}") for i in range(RINGW)]
        silu_ready, used, added = st.sem("silu"), st.sem("used"), st.sem("added")
        stored, padded, silu_tr, silu_col, stream = (st.sem(x) for x in ("stored", "padded", "silutr", "silucol", "stream"))
        with nc.Block() as block:
            @block.sync
            def _(sp):
                for k in range(2):
                    sp.dma_start(cond[KD * k:KD * k + KD], (m.c if k == 0 else m.c_ctx).rearrange(
                        "(k p) -> k p", p=P)).then_inc(conds, 16)
                sp.dma_start(m.small[:, :], m.c_small).then_inc(consts, 16)
                for c in range(NC):
                    if c >= RINGW:
                        sp.wait_ge(used, c - RINGW + 1)
                    sp.dma_start(w[:, c % RINGW], m.ada_w[0].rearrange("(k p) n -> p k n", p=P)[
                        :, :, c * 512:(c + 1) * 512]).then_inc(ada[c % RINGW], 16)
                sp.wait_ge(added, NC)
                sp.dma_start(m.mods[0], rows[:]).then_inc(stored, 16)
                sp.wait_ge(stored, 16)

            @block.scalar
            def _(act):
                for k in range(2):
                    act.dma_start(rows[k:k + 1], m.ada_b[0:1]).then_inc(biases, 16)
                act.wait_ge(conds, 32)
                nc.scalar.activation(silu_rows[:], cond[:], ACT.Silu).then_inc(silu_ready, 1)
                act.wait_ge(padded, 1)
                act.dma_start(pad[:, 48:79], m.rpb.rearrange("l h r c -> (l h r) c")).then_inc(rpb, 16)
                act.wait_ge(rpb, 16)
                act.dma_start(m.rpb_pad, bcast(pad[:], 1, GRID_W)).then_inc(rpb, 16)
                act.wait_ge(used, NC // 2)
                act.dma_start(m.X[:, 0:CT, :], m.ctx.rearrange("(t p) d -> p t d", p=P)).then_inc(stream, 16)
                act.dma_start(m.X[:, CT:NT, :], m.x.rearrange("(t p) d -> p t d", p=P)).then_inc(stream, 16)
                act.wait_ge(rpb, 32)
                act.wait_ge(stream, 32)

            @block.tensor
            def _(pe):
                pe.wait_ge(silu_ready, 1)
                pe.wait_ge(consts, 16)
                nc.tensor.transpose(tr[:, 0:2 * KD], silu_rows[:], m.small[0:2 * KD, 0:2 * KD]).then_inc(silu_tr, 1)
                pe.wait_ge(silu_col, 1)
                for c in range(NC):
                    pe.wait_ge(ada[c % RINGW], 16 * (c // RINGW + 1))
                    if c >= 4:
                        pe.wait_ge(added, c - 3)
                    for k in range(KD):
                        mm = nc.tensor.matmul(acc[0:2, c % 4], m.silu[:, :, k], w[:, c % RINGW, k],
                                              start=k == 0, stop=k == KD - 1)
                    mm.then_inc(used, 1)

            @block.vector
            def _(dve):
                nc.vector.memset(pad[:], 0.0).then_inc(padded, 1)
                dve.wait_ge(silu_tr, 1)
                nc.vector.tensor_copy(m.silu[:].rearrange("p s k -> p (s k)"), tr[:, 0:2 * KD]).then_inc(silu_col, 1)
                dve.wait_ge(biases, 32)
                for c in range(NC):
                    dve.wait_ge(used, c + 1)
                    row = rows[:, c * 512:(c + 1) * 512]
                    nc.vector.tensor_tensor(row, row, acc[0:2, c % 4], ALU.add).then_inc(added, 1)


def mod_row(m, l, ctx, which):
    return m.mods[l].rearrange("s (w d) -> s w d", w=6)[ctx, which]


def norm_modulate(nc, m, l, gain, which, t0, HT, st, block, ht, rows_of, H=None, after=None, squares=True):
    sc, sh, g, junk = rows_of[:, 0:2], rows_of[:, 2:4], rows_of[:, 4], rows_of[:, 5]
    stat = st.sb("stat", [P, 4, NT])
    own = H is None
    h = st.sb("h", [P, 2, D]) if own else H
    tr = st.ps("htr", [P, 2, 2, 512])
    rows, ssq, mean, root, inv = (st.sem(x) for x in ("mod_rows", "ssq", "mean", "root", "inv"))
    coef, hs, hb, trs, shifts = (st.sem(x) for x in ("coef", "hscaled", "h", "htr", "shifts"))
    ev0, ev1 = ht
    tiles = list(range(t0, NT))
    n = len(tiles)
    streams = [0, 1] if t0 < CT else [1]

    @block.sync
    def _(sp):
        sp.dma_start(g, row_bcast(gain)).then_inc(rows, 16)
        for s in streams:
            sp.dma_start(sc[:, s], row_bcast(mod_row(m, l, 1 - s, which + 1))).then_inc(rows, 16)
        for s in streams:
            sp.dma_start(sh[:, s], row_bcast(mod_row(m, l, 1 - s, which))).then_inc(shifts, 16)

    @block.scalar
    def _(act):
        for i, t in enumerate(tiles if squares else []):
            if i:
                act.wait_ge(ssq, i)
            nc.scalar.activation(junk, m.X[:, t], ACT.Square, accum_out=m.ssq[:, t:t + 1]).then_inc(ssq, 1)
        act.wait_ge(mean, 1)
        nc.scalar.activation(stat[:, 2, t0:NT], stat[:, 1, t0:NT], ACT.Sqrt).then_inc(root, 1)
        for i, t in enumerate(tiles):
            act.wait_ge(trs, i + 1)
            nc.scalar.activation(HT[:, 0:4, t * P:(t + 1) * P], tr[:, i % 2, 0].rearrange("p (k n) -> p k n", n=P),
                                 ACT.Copy).then_inc(ev0, 1)

    @block.vector
    def _(dve):
        def coefficients():
            dve.wait_ge(rows, 16 * (1 + len(streams)))
            for s in streams:
                nc.vector.scalar_tensor_tensor(out=sc[:, s], in0=sc[:, s], scalar=1.0, in1=g,
                                               op0=ALU.add, op1=ALU.mult).then_inc(coef, 1)

        if squares:
            coefficients()
            dve.wait_ge(ssq, n)
        nc.vector.tensor_scalar(stat[:, 1, t0:NT], m.ssq[:, t0:NT], 1.0 / D, EPS, ALU.mult, ALU.add).then_inc(mean, 1)
        dve.wait_ge(root, 1)
        nc.vector.reciprocal(stat[:, 3, t0:NT], stat[:, 2, t0:NT]).then_inc(inv, 1)
        if not squares:
            coefficients()
        dve.wait_ge(inv, 1)
        dve.wait_ge(coef, len(streams))

        def evacuate(i):
            t = tiles[i]
            dve.wait_ge(trs, i + 1)
            nc.vector.tensor_copy(HT[:, 4:8, t * P:(t + 1) * P],
                                  tr[:, i % 2, 1].rearrange("p (k n) -> p k n", n=P)).then_inc(ev1, 1)

        for i, t in enumerate(tiles):
            if own and i >= 2:
                dve.wait_ge(trs, i - 1)
            nc.vector.scalar_tensor_tensor(out=h[:, i % 2 if own else t], in0=m.X[:, t], scalar=stat[:, 3, t:t + 1],
                                           in1=sc[:, 0 if t < CT else 1], op0=ALU.mult, op1=ALU.mult).then_inc(hs, 1)
            if i:
                evacuate(i - 1)
        evacuate(n - 1)

    @block.gpsimd
    def _(pool):
        pool.wait_ge(shifts, 16 * len(streams))
        for i, t in enumerate(tiles):
            pool.wait_ge(hs, i + 1)
            b = i % 2 if own else t
            nc.gpsimd.tensor_tensor(h[:, b], h[:, b], sh[:, 0 if t < CT else 1], ALU.add).then_inc(hb, 1)

    @block.tensor
    def _(pe):
        for i, t in enumerate(tiles):
            pe.wait_ge(hb, i + 1)
            if i >= 2:
                pe.wait_ge(ev0, i - 1)
                pe.wait_ge(ev1, i - 1)
            for k in range(KD):
                mm = nc.tensor.transpose(tr[:, i % 2, k // 4, (k % 4) * P:(k % 4 + 1) * P],
                                         h[:, i % 2 if own else t, k * P:(k + 1) * P], m.ident)
            mm.then_inc(trs, 1)
            if after is not None:
                after(pe, i)

def project(nc, m, l, HT, PR, scratch):
    last = l == DEPTH - 1
    WR, BANKS = 2, 4
    with Stage(nc, f"proj{l}") as st:
        w = st.sb("w", [P, WR, KD, 512])
        acc = st.ps("acc", [P, BANKS, 512])
        ws = [st.sem(f"w{i}") for i in range(WR)]
        prods, ev = st.sem("prods"), st.sem("ev")
        ht = st.sem("ht0"), st.sem("ht1")
        work = [(c, t) for c, (_, _, need) in enumerate(PROJ_CHUNKS) for t in range(NT) if need or not last or t >= CT]
        with nc.Block() as block:
            def product(pe, i):
                c, t = work[i]
                wd = PROJ_CHUNKS[c][1]
                if i < NT:
                    pe.wait_ge(ht[0], t + 1)
                    pe.wait_ge(ht[1], t + 1)
                if i == 0 or work[i - 1][0] != c:
                    pe.wait_ge(ws[c % WR], 16 * (c // WR + 1))
                if i >= BANKS:
                    pe.wait_ge(ev, i - BANKS + 1)
                for k in range(KD):
                    mm = nc.tensor.matmul(acc[:, i % BANKS, 0:wd], HT[:, k, t * P:(t + 1) * P], w[:, c % WR, k, 0:wd],
                                          start=k == 0, stop=k == KD - 1)
                mm.then_inc(prods, 1)

            def early(pe, i):
                if i:
                    product(pe, i - 1)

            norm_modulate(nc, m, l, m.a["norm1_g"][l], 0, 0, HT, st, block, ht, scratch, after=early)

            @block.sync
            def _(sp):
                for c, (c0, wd, _) in enumerate(PROJ_CHUNKS):
                    if c >= WR:
                        sp.wait_ge(prods, sum(x[0] <= c - WR for x in work))
                    sp.dma_start(w[:, c % WR, :, 0:wd], m.w_in[l].rearrange("(k p) n -> p k n", p=P)[
                        :, :, c0:c0 + wd]).then_inc(ws[c % WR], 16)

            @block.tensor
            def _(pe):
                for i in range(NT - 1, len(work)):
                    product(pe, i)

            @block.vector
            def _(dve):
                for i, (c, t) in enumerate(work):
                    c0, wd, _ = PROJ_CHUNKS[c]
                    dve.wait_ge(prods, i + 1)
                    nc.vector.tensor_copy(PR[:, t, c0:c0 + wd], acc[:, i % BANKS, 0:wd]).then_inc(ev, 1)


SMALL = P + 256 + GRID_W + 16
_INS = ["x", "c", "ctx", "c_ctx", "ada_w", "ada_b", "norm1_g", "norm2_g", "w_in", "gla_gate_up", "gla_gate_b",
        "gla_norm_g", "nat_rpb", "diff_lambda", "diff_norm_g", "w_out", "peer_wq", "peer_subkeys", "peer_u",
        "peer_v", "final_g"]


def build(nc, a, out, stop=None, keep=None):
    m = Model()
    m.x, m.ctx = a["x"].rearrange("b t d -> (b t) d"), a["ctx"].rearrange("b t d -> (b t) d")
    m.c, m.c_ctx = a["c"].rearrange("b d -> (b d)"), a["c_ctx"]
    m.ada_w, m.ada_b, m.rpb, m.w_in = a["ada_w"], a["ada_b"], a["nat_rpb"], a["w_in"]
    m.c_small, m.c_rope, m.c_levels = a["small"], a["rope"], a["levels"]
    m.a = a
    m.mods = nc.dram_tensor("mods", (DEPTH, 2, 6 * D), F32, kind="Internal").ap()
    m.rpb_pad = nc.dram_tensor("rpb_pad", (DEPTH * HEADS * 15, GRID_W, P), F32, kind="Internal").ap()
    with ExitStack() as ctx:
        def sb(name, shape, dt=F32):
            return ctx.enter_context(nc.sbuf_tensor(name, shape, dt))
        m.X = sb("X", [P, NT, D])
        m.silu = sb("silu", [P, 2, KD])
        m.ssq = sb("ssq", [P, NT])
        m.rstat = sb("rstat", [P, 4, NT * HEADS])
        m.small = sb("small", [P, SMALL])
        m.ident = m.small[:, 0:P]
        m.block = m.small[:, P:P + 256]
        m.window = m.small[:, P + 256:P + 256 + GRID_W]
        m.iota = m.small[:, P + 256 + GRID_W:SMALL]
        m.ug = [ctx.enter_context(nc.semaphore(f"u_rows{i}")) for i in range(RING)]
        m.vg = [ctx.enter_context(nc.semaphore(f"v_rows{i}")) for i in range(RING)]
        setup(nc, m)
        for l in range(DEPTH):
            layer(nc, m, l, stop)
            if stop is not None:
                return
        finish(nc, m, out)


def layer(nc, m, l, stop):
    t0 = CT if l == DEPTH - 1 else 0
    with nc.sbuf_tensor(f"Y{l}", [P, NT, D], F32) as Y:
        with nc.sbuf_tensor(f"PR{l}", [P, NT, PROJ], F32) as PR:
            with nc.sbuf_tensor(f"HT{l}", [P, KD, TOK], F32) as HT:
                project(nc, m, l, HT, PR, Y)
                if stop == "proj":
                    return
            gla(nc, m, l, PR, Y)
            if stop == "gla":
                return
            neighbourhood(nc, m, l, PR, Y)
            if stop == "nat":
                return
            differential(nc, m, l, PR, Y)
            if stop == "diff":
                return
        out_project(nc, m, l, t0, Y)
        if stop == "out":
            return
    peer(nc, m, l, t0)


def bcast(ap, at, n):
    dims = [list(x) for x in ap.ap]
    return bass.AP(ap.tensor, ap.offset, dims[:at] + [[0, n]] + dims[at:])


def stretch(ap, n):
    dims = [list(x) for x in ap.ap]
    assert dims[-1][1] == 1
    return bass.AP(ap.tensor, ap.offset, dims[:-1] + [[0, n]])


def gla(nc, m, l, PR, Y):
    t0 = CT if l == DEPTH - 1 else 0
    n_out = NT - t0
    orders = [[0, 1, 2, 3, 4, 5], [1, 0, 5, 4, 3, 2]]
    with ExitStack() as ctx:
        def sb(name, shape):
            return ctx.enter_context(nc.sbuf_tensor(f"gla{l}_{name}", shape, F32))
        QT, KT = sb("QT", [P, TOK]), sb("KT", [P, TOK])
        B = sb("B", [P, 2, NT, P + 1])
        QW = sb("QW", [P, 2, TOK])
        S = sb("S", [P, 2, NT, 256])
        gla_gates(nc, m, l, PR, QT, KT, B, QW, S, orders)
        gla_scores(nc, m, l, t0, PR, Y, QT, KT, B, QW, S, orders)


def gla_gates(nc, m, l, PR, QT, KT, B, QW, S, orders):
    with Stage(nc, f"gates{l}") as st:
        up, brow, bcol = st.sb("up", [16, 2, P]), st.sb("brow", [2, P]), st.sb("bcol", [P, 2])
        GT = st.sb("GT", [16, 2, TOK])
        a, e, g = st.sb("a", [P, 2, TOK]), st.sb("e", [P, 2, TOK]), st.sb("g", [P, 2, TOK])
        ones, tot = st.sb("ones", [P, P]), st.sb("tot", [P, 2, NT])
        KW, KN = st.sb("KW", [P, 2, TOK]), st.sb("KN", [P, 2, NT, P])
        U = st.sb("U", [P, 2, 256])
        tr = st.ps("tr", [P, 2, 512])
        Z = st.ps("Z", [P, 2, 1024])
        acc = st.ps("acc", [P, 2, 512])
        small, btr, bready, trs, qk, evq, evk, evg, zs = (st.sem(x) for x in (
            "small", "btr", "bready", "trs", "qk", "evq", "evk", "evg", "zs"))
        lns, expd, expw, gs, minz, kw, ktr, kn, us, upd, chain, aux, args = (st.sem(x) for x in (
            "lns", "expd", "expw", "gs", "minz", "kw", "ktr", "kn", "us", "upd", "chain", "aux", "args"))
        zbs = st.sem("zbs")
        steps = [(d, n) for n in range(NT - 1) for d in range(2)]
        with nc.Block() as block:
            @block.sync
            def _(sp):
                sp.dma_start(up[:], m.a["gla_gate_up"][l].rearrange("d r c -> r d c")).then_inc(small, 16)
                sp.dma_start(brow[:], m.a["gla_gate_b"][l]).then_inc(small, 16)

            @block.tensor
            def _(pe):
                pe.wait_ge(small, 32)
                nc.tensor.transpose(acc[:, 0, 0:2], brow[:], m.small[0:2, 0:2]).then_inc(btr, 1)
                for t in range(NT):
                    if t >= 2:
                        pe.wait_ge(evq, t - 1)
                        pe.wait_ge(evk, t - 1)
                        pe.wait_ge(evg, t - 1)
                    nc.tensor.transpose(tr[:, t % 2, 0:P], PR[:, t, GQ:GQ + P], m.ident)
                    nc.tensor.transpose(tr[:, t % 2, P:2 * P], PR[:, t, GK:GK + P], m.ident)
                    for d in range(2):
                        mm = nc.tensor.transpose(tr[0:16, t % 2, (2 + d) * P:(3 + d) * P],
                                                 PR[:, t, GG + 16 * d:GG + 16 * d + 16], m.ident)
                    mm.then_inc(trs, 1)
                pe.wait_ge(evg, NT)
                for d in range(2):
                    nc.tensor.matmul(Z[:, d, 0:512], up[:, d], GT[:, d, 0:512], start=True, stop=True)
                    nc.tensor.matmul(Z[:, d, 512:TOK], up[:, d], GT[:, d, 512:TOK], start=True, stop=True).then_inc(zs, 1)
                def turn(i):
                    d, n = steps[i]
                    t = orders[d][n]
                    pe.wait_ge(kw, d + 1)
                    if i >= 2:
                        pe.wait_ge(kn, i - 1)
                    nc.tensor.transpose(tr[:, i % 2, 0:P], KW[:, d, t * P:(t + 1) * P], m.ident).then_inc(ktr, 1)

                turn(0)
                for i, (d, n) in enumerate(steps):
                    t = orders[d][n]
                    if i + 1 < len(steps):
                        turn(i + 1)
                    pe.wait_ge(kn, i + 1)
                    if i >= 2:
                        pe.wait_ge(us, i - 1)
                    nc.tensor.matmul(acc[:, i % 2, 0:256], KN[:, d, t], PR[:, t, GV:GV + 256],
                                     start=True, stop=True).then_inc(upd, 1)

            @block.scalar
            def _(act):
                for t in range(NT):
                    act.wait_ge(trs, t + 1)
                    act.wait_ge(evg, t + 1)
                    nc.scalar.activation(KT[:, t * P:(t + 1) * P], tr[:, t % 2, P:2 * P], ACT.Copy).then_inc(evk, 1)
                n = 0
                for d in range(2):
                    act.wait_ge(zbs, d + 1)
                    nc.scalar.activation(a[:, d], g[:, d], ACT.Abs).then_inc(aux, 1)
                    act.wait_ge(aux, n + 1)
                    nc.scalar.activation(e[:, d], a[:, d], ACT.Exp, scale=-1.0).then_inc(aux, 1)
                    act.wait_ge(aux, n + 2)
                    nc.scalar.activation(e[:, d], e[:, d], ACT.Ln, bias=1.0).then_inc(lns, 1)
                    n += 2
                for d in range(2):
                    act.wait_ge(args, d + 1)
                    first, second = B[:, d, :, 1 - d:P + 1 - d], a[:, d].rearrange("p (t s) -> p t s", s=P)
                    e3, g3 = (x[:, d].rearrange("p (t s) -> p t s", s=P) for x in (e, g))
                    nc.scalar.activation(e3, first, ACT.Exp, scale=1.0 / TAU).then_inc(expw, 1)
                    nc.scalar.activation(g3, second, ACT.Exp, scale=1.0 / TAU).then_inc(expw, 1)
                    nc.scalar.activation(tot[:, d], B[:, d, :, P], ACT.Exp, scale=1.0 / TAU).then_inc(expd, 1)
                for i, (d, n) in enumerate(steps):
                    act.wait_ge(ktr, i + 1)
                    nc.scalar.activation(KN[:, d, orders[d][n]], tr[:, i % 2, 0:P], ACT.Copy).then_inc(kn, 1)

            @block.vector
            def _(dve):
                link = linker(dve, chain)
                nc.vector.memset(ones[:], 1.0)
                nc.vector.memset(B[:, :, :, 0:1], 0.0)
                link(nc.vector.memset(S[:, :, 0], 0.0))
                dve.wait_ge(btr, 1)
                nc.vector.tensor_copy(bcol[:], acc[:, 0, 0:2]).then_inc(bready, 1)
                for t in range(NT):
                    dve.wait_ge(trs, t + 1)
                    nc.vector.tensor_scalar(QT[:, t * P:(t + 1) * P], tr[:, t % 2, 0:P], 32 ** -0.5, None, ALU.mult).then_inc(evq, 1)
                    nc.vector.tensor_copy(GT[:, :, t * P:(t + 1) * P], tr[0:16, t % 2, 2 * P:4 * P].rearrange(
                        "p (d n) -> p d n", d=2)).then_inc(evg, 1)
                dve.wait_ge(bready, 1)
                for d in range(2):
                    dve.wait_ge(zs, d + 1)
                    nc.vector.tensor_scalar(g[:, d], Z[:, d, 0:TOK], bcol[:, d:d + 1], None, ALU.add).then_inc(zbs, 1)
                for d in range(2):
                    dve.wait_ge(lns, d + 1)
                    link(nc.vector.scalar_tensor_tensor(out=g[:, d], in0=g[:, d], scalar=0.0, in1=e[:, d],
                                                        op0=ALU.min, op1=ALU.subtract))
                    for t in range(NT):
                        ins = nc.vector.tensor_tensor_scan(B[:, d, t, 1:P + 1], ones[:], g[:, d, t * P:(t + 1) * P], 0.0,
                                                           ALU.mult, ALU.add)
                    link(ins)
                    nc.vector.tensor_tensor(a[:, d].rearrange("p (t s) -> p t s", s=P),
                                            stretch(B[:, d, :, P:P + 1], P), B[:, d, :, 1 - d:P + 1 - d],
                                            ALU.subtract).then_inc(args, 1)
                dve.wait_ge(evq, NT)
                dve.wait_ge(evk, NT)
                for d in range(2):
                    entry, exit_ = (e, g) if d == 0 else (g, e)
                    dve.wait_ge(expw, 2 * d + 2)
                    nc.vector.tensor_tensor(KW[:, d], KT[:], exit_[:, d], ALU.mult).then_inc(kw, 1)
                    nc.vector.tensor_tensor(QW[:, d], QT[:], entry[:, d], ALU.mult)
                dve.wait_ge(expd, 2)
                for i, (d, n) in enumerate(steps):
                    t = orders[d][n]
                    dve.wait_ge(upd, i + 1)
                    nc.vector.tensor_tensor(U[:, d], acc[:, i % 2, 0:256], m.block, ALU.mult).then_inc(us, 1)
                    dve.wait_ge(us, i + 1)
                    link(nc.vector.scalar_tensor_tensor(out=S[:, d, n + 1], in0=S[:, d, n], scalar=tot[:, d, t:t + 1],
                                                        in1=U[:, d], op0=ALU.mult, op1=ALU.add))


def gla_scores(nc, m, l, t0, PR, Y, QT, KT, B, QW, S, orders):
    tiles = [(d, t) for d in range(2) for t in range(t0, NT)]
    n_dir = NT - t0
    BANKS = 6
    POOL_HEADS = 2
    with Stage(nc, f"glascore{l}") as st:
        levels = st.sb("levels", [P, NLEV, P])
        masks = st.sb("masks", [P, 2, NLEV, P], U8)
        K = st.sb("K", [P, 3, NLEV - 1, P])
        Q = st.sb("Q", [P, 2, NLEV, HEADS, P])
        A = st.sb("A", [P, 2, HEADS, P])
        sc = st.ps("sc", [P, BANKS, 512])
        O = st.ps("O", [P, 2, 512])
        qown, loaded = st.sem("qown"), st.sem("loaded")
        masked, zeroed, subs, absd, decays, khat, qhat, qdiag, scs, cps, outs, ev0, ev1 = (st.sem(x) for x in (
            "masks", "zeroed", "subs", "absd", "decays", "khat", "qhat", "qdiag", "scores", "copies", "outs", "ev0", "ev1"))
        head_rows = [slice(32 * h, 32 * h + 32) for h in range(HEADS)]
        with nc.Block() as block:
            @block.sync
            def _(sp):
                for d in range(2):
                    if d:
                        sp.wait_ge(masked, d)
                    sp.dma_start(levels[:], m.c_levels.rearrange("p (d n i) -> p d n i", d=2, n=NLEV)[:, d]).then_inc(loaded, 16)

            @block.scalar
            def _(act):
                def decay(n):
                    F = K[:, n % 3]
                    act.wait_ge(subs, (n + 1) * len(LEVELS))
                    nc.scalar.activation(F, F, ACT.Abs).then_inc(absd, 1)
                    act.wait_ge(absd, n + 1)
                    nc.scalar.activation(F, F, ACT.Exp, scale=-1.0 / TAU).then_inc(decays, 1)

                def diagonal(n):
                    t = tiles[n][1]
                    if n == 0:
                        act.wait_ge(zeroed, 1)
                    if n >= 2:
                        act.wait_ge(scs, NLEV * (n - 1))
                    for h, rows in enumerate(head_rows):
                        ins = nc.scalar.activation(Q[rows, n % 2, NLEV - 1, h], QT[rows, t * P:(t + 1) * P], ACT.Copy)
                    ins.then_inc(qdiag, 1)

                decay(0)
                decay(1)
                for d in range(2):
                    act.wait_ge(loaded, 16 * (d + 1))
                    nc.scalar.activation(masks[:, d], levels[:], ACT.Copy).then_inc(masked, 1)
                    if d == 0:
                        diagonal(0)
                for n, (d, t) in enumerate(tiles):
                    if n + 1 < len(tiles):
                        diagonal(n + 1)
                    if n + 2 < len(tiles):
                        decay(n + 2)
                    if d == 0:
                        act.wait_ge(outs, n + 1)
                        nc.scalar.activation(Y[:, t, 0:256], O[:, n % 2, 0:256], ACT.Copy).then_inc(ev0, 1)

            @block.gpsimd
            def _(pool):
                nc.gpsimd.memset(Q[:], 0.0).then_inc(zeroed, 1)
                pool.wait_ge(zeroed, 1)
                for n, (d, t) in enumerate(tiles):
                    pool.wait_ge(decays, n + 1)
                    if n >= 2:
                        pool.wait_ge(scs, NLEV * (n - 1))
                    for h, rows in enumerate(head_rows[:POOL_HEADS]):
                        if n or h:
                            pool.wait_ge(qhat, POOL_HEADS * n + h)
                        nc.gpsimd.tensor_tensor(Q[rows, n % 2, 0:NLEV - 1, h], K[rows, n % 3],
                                                bcast(QT[rows, t * P:(t + 1) * P], 1, NLEV - 1), ALU.mult).then_inc(qhat, 1)
                    pool.wait_ge(qown, n + 1)
                    pool.wait_ge(qhat, POOL_HEADS * (n + 1))
                    nc.gpsimd.tensor_tensor(K[:, n % 3], K[:, n % 3], bcast(KT[:, t * P:(t + 1) * P], 1, NLEV - 1),
                                            ALU.mult).then_inc(khat, 1)

            @block.tensor
            def _(pe):
                def output(n):
                    d, t = tiles[n]
                    pe.wait_ge(cps, NLEV * (n + 1))
                    if n >= 2:
                        pe.wait_ge(*((ev0, n - 1) if n - 2 < n_dir else (ev1, n - 1 - n_dir)))
                    nc.tensor.matmul(O[:, n % 2, 0:256], QW[:, d, t * P:(t + 1) * P], S[:, d, orders[d].index(t)],
                                     start=True, stop=False, skip_group_check=True)
                    for h in range(HEADS):
                        mm = nc.tensor.matmul(O[:, n % 2, 64 * h:64 * h + 64], A[:, n % 2, h], PR[:, t, GV + 64 * h:GV + 64 * h + 64],
                                              start=False, stop=h == HEADS - 1, skip_group_check=True)
                    mm.then_inc(outs, 1)

                for n, (d, t) in enumerate(tiles):
                    pe.wait_ge(khat, n + 1)
                    pe.wait_ge(qdiag, n + 1)
                    for lv in range(NLEV):
                        k = n * NLEV + lv
                        if k >= BANKS:
                            pe.wait_ge(cps, k - BANKS + 1)
                        keys = K[:, n % 3, lv] if lv < NLEV - 1 else KT[:, t * P:(t + 1) * P]
                        nc.tensor.matmul(sc[:, k % BANKS], keys, Q[:, n % 2, lv].rearrange("p h i -> p (h i)"),
                                         start=True, stop=True).then_inc(scs, 1)
                    if n:
                        output(n - 1)
                output(len(tiles) - 1)

            @block.vector
            def _(dve):
                def difference(n, lv):
                    d, t = tiles[n]
                    s = LEVELS[lv]
                    if n >= 3 and lv == 0:
                        dve.wait_ge(scs, NLEV * (n - 2))
                    b = B[:, d, t, 1 - d:P + 1 - d].rearrange("p (n s) -> p n s", s=2 * s)
                    border = b[:, :, s - 1:s] if d == 0 else b[:, :, s:s + 1]
                    nc.vector.tensor_tensor(K[:, n % 3, lv].rearrange("p (n s) -> p n s", s=2 * s),
                                            b, stretch(border, 2 * s), ALU.subtract).then_inc(subs, 1)

                def queries(n):
                    t = tiles[n][1]
                    dve.wait_ge(decays, n + 1)
                    if n == 0:
                        dve.wait_ge(zeroed, 1)
                    for h in range(POOL_HEADS, HEADS):
                        rows = head_rows[h]
                        ins = nc.vector.tensor_tensor(Q[rows, n % 2, 0:NLEV - 1, h], K[rows, n % 3],
                                                      bcast(QT[rows, t * P:(t + 1) * P], 1, NLEV - 1), ALU.mult)
                    ins.then_inc(qown, 1)

                def evacuate(n):
                    d, t = tiles[n]
                    if d == 1:
                        dve.wait_ge(outs, n + 1)
                        if n == n_dir:
                            dve.wait_ge(ev0, n_dir)
                        nc.vector.tensor_tensor(Y[:, t, 0:256], Y[:, t, 0:256], O[:, n % 2, 0:256], ALU.add).then_inc(ev1, 1)

                for n in range(2):
                    for lv in range(NLEV - 1):
                        difference(n, lv)
                queries(0)
                dve.wait_ge(masked, 2)
                for n, (d, t) in enumerate(tiles):
                    if n >= 2:
                        dve.wait_ge(outs, n - 1)
                    for lv in range(NLEV):
                        k = n * NLEV + lv
                        dve.wait_ge(scs, k + 1)
                        src = sc[:, k % BANKS].rearrange("p (h i) -> p h i", h=HEADS)
                        mask = bcast(masks[:, d, lv], 1, HEADS)
                        if lv == 0:
                            nc.vector.tensor_tensor(A[:, n % 2], src, mask, ALU.mult).then_inc(cps, 1)
                        else:
                            dve.wait_ge(cps, k)
                            nc.vector.copy_predicated(A[:, n % 2], mask, src).then_inc(cps, 1)
                        if lv < NLEV - 1 and n + 2 < len(tiles):
                            difference(n + 2, lv)
                        if lv == 2 and n + 1 < len(tiles):
                            queries(n + 1)
                    if n:
                        evacuate(n - 1)
                evacuate(len(tiles) - 1)


def neighbourhood(nc, m, l, PR, Y):
    attention(nc, m, l, PR, Y, "nat")


def differential(nc, m, l, PR, Y):
    attention(nc, m, l, PR, Y, "diff")


def attention(nc, m, l, PR, Y, kind):
    diff = kind == "diff"
    maps = 2 if diff else 1
    last = l == DEPTH - 1
    CQ = 4 if diff else 2
    q0, k0, v0 = (DQ, DK, DV) if diff else (NQ, NK, NV)
    dv = 128 if diff else 64
    y0 = 512 if diff else 256
    tq = CT if last else 0
    units = [(t, h) for t in range(tq, NT) for h in range(HEADS)]
    keys = [TOK if t >= CT else CTX for t, _ in units]
    wide = [int(n == TOK) for n in keys]
    N = len(units)
    first_wide = wide.index(1)
    with Stage(nc, f"{kind}{l}") as st:
        QT, KT = st.sb("QT", [P, CQ, 2, TOK]), st.sb("KT", [P, CQ, TOK])
        E = st.sb("E", [P, 2, maps, TOK])
        AT = st.sb("AT", [P, 2, TOK])
        stat = st.sb("stat", [P, 3, 16])
        S = st.ps("S", [P, 2, 1024])
        tr = st.ps("tr", [P, 2, 512])
        O = st.ps("O", [P, 2, 512])
        names = ("prep", "evq", "evk", "scores", "negs", "exps", "sums", "chain", "probs", "trs", "eva", "evb", "outs",
                 "oev")
        prep, evq, evk, scores, negs, exps, sums, chain, probs, trs, eva, evb, outs, oev = (st.sem(x) for x in names)
        loads, zeroed = st.sem("loads"), st.sem("zeroed")
        if diff:
            lam = st.sb("lam", [P, 4, 64])
            lamv = st.sb("lamv", [P, 8])
            rstat = m.rstat
            sq = st.sb("sq", [P, P])
            lams, lexp = st.sem("lams"), st.sem("lexp")
        else:
            bias = st.sb("bias", [P, HEADS, 16, GRID_W])
            SB = st.sb("SB", [P, 2, SEQ])
            rope = st.sb("rope", [P, LT, P])
            r1, r2 = st.sb("r1", [P, 512]), st.sb("r2", [P, 512])
            G_STEPS, SILU_AT, ROOT_AT = range(2, 9), 1, 6
            n_out = NT - tq
            g_gain, g_silu, g_sq = st.sb("ggain", [P, 256]), st.sb("gsilu", [P, NT, 256]), st.sb("gsq", [P, NT, 256])
            g_stat = st.sb("gstat", [P, 4, NT * HEADS])
            g_gains, g_silus, g_chain, g_mean, g_root = (st.sem(x) for x in ("ggains", "gsilus", "gchain", "gmean", "groot"))
            rotary, biases, biased, pchain = st.sem("rotary"), st.sem("biases"), st.sem("biased"), st.sem("pchain")

        with nc.Block() as block:
            @block.sync
            def _(sp):
                if diff:
                    sp.dma_start(lam[:].rearrange("p a b -> p (a b)"), row_bcast(
                        m.a["diff_lambda"][l:l + 1].rearrange("l a b -> l (a b)")[0])).then_inc(loads, 16)
                    return
                sp.dma_start(g_gain[:], row_bcast(m.a["gla_norm_g"][l])).then_inc(g_gains, 16)
                sp.dma_start(rope[:], m.c_rope.rearrange("(t p) c -> p t c", p=P)).then_inc(rotary, 16)
                row = m.rpb_pad[0:1]
                for half in range(2):
                    for h in range(HEADS):
                        src = bass.AP(row.tensor, (l * HEADS + h) * 15 * GRID_W * P + GRID_W - 1, [[P - 1, GRID_W], [GRID_W * P, 15], [1, GRID_W]])
                        sp.dma_start(bias[GRID_W * half:GRID_W * half + GRID_W, h, half:half + 15], src).then_inc(biases, 16)

            @block.gpsimd
            def _(pool):
                if diff:
                    return
                link = linker(pool, pchain)
                pool.wait_ge(biases, 128)
                b = bias[:, :, 1:15]
                for h in range(HEADS):
                    nc.gpsimd.tensor_tensor(b[:, h], b[:, h], bcast(m.window, 1, 14), ALU.add).then_inc(biased, 1)
                pool.wait_ge(rotary, 16)
                for t in range(CT, NT):
                    cos = bcast(rope[:, t - CT, 0:64], 1, 8)
                    sin = rope[:, t - CT, 64:128].rearrange("p (a h f) -> p a h f", a=2, h=2)
                    for c0 in (DQ, DK):
                        x = PR[:, t, c0:c0 + 512]
                        xm = x.rearrange("p (g f) -> p g f", f=64)
                        nc.gpsimd.tensor_tensor(r1[:].rearrange("p (g f) -> p g f", f=64), xm, cos, ALU.mult)
                        for half in range(2):
                            src = x.rearrange("p (g a h f) -> p g a h f", g=8, a=2, h=2)[:, :, :, 1 - half]
                            dst = r2[:].rearrange("p (g a h f) -> p g a h f", g=8, a=2, h=2)[:, :, :, half]
                            ins = nc.gpsimd.tensor_tensor(dst, src, bcast(sin[:, :, half], 1, 8), ALU.mult)
                        link(ins)
                        link(nc.gpsimd.tensor_tensor(x, r1[:], r2[:], ALU.add))

            @block.tensor
            def _(pe):
                for t in range(NT):
                    if t >= 2:
                        pe.wait_ge(evq, t - 1)
                        pe.wait_ge(evk, t - 1)
                    for c in range(CQ):
                        mm = nc.tensor.transpose(S[:, t % 2, 512 + c * P:512 + (c + 1) * P], PR[:, t, k0 + c * P:k0 + (c + 1) * P], m.ident)
                    for c in range(CQ if t >= tq else 0):
                        mm = nc.tensor.transpose(S[:, t % 2, c * P:(c + 1) * P], PR[:, t, q0 + c * P:q0 + (c + 1) * P], m.ident)
                    mm.then_inc(prep, 1)
                pe.wait_ge(evq, NT)
                pe.wait_ge(evk, NT)
                pe.wait_ge(zeroed, 2)

                def score(u):
                    t, h = units[u]
                    for j in range(maps):
                        g = maps * u + j
                        if g >= 2:
                            pe.wait_ge(exps, g - 1)
                        c, half = (h, j) if diff else (h // 2, h % 2)
                        q = QT[:, c, half, t * P:(t + 1) * P]
                        for a, b in ((0, 512), (512, TOK)) if wide[u] else ((0, CTX),):
                            mm = nc.tensor.matmul(S[:, g % 2, a:b], q, KT[:, c, a:b], start=True, stop=True)
                        mm.then_inc(scores, 1)

                def output(u):
                    t, h = units[u]
                    pe.wait_ge(eva, u + 1)
                    if wide[u]:
                        pe.wait_ge(evb, sum(wide[:u + 1]))
                    if u >= 2:
                        pe.wait_ge(oev, u - 1)
                    nk = keys[u] // P
                    for c in range(nk):
                        mm = nc.tensor.matmul(O[:, u % 2, 0:dv], AT[:, u % 2, c * P:(c + 1) * P],
                                              PR[:, c, v0 + h * dv:v0 + (h + 1) * dv], start=c == 0, stop=c == nk - 1)
                    mm.then_inc(outs, 1)

                score(0)
                for u, (t, h) in enumerate(units):
                    if u + 1 < N:
                        score(u + 1)
                    pe.wait_ge(probs if diff else exps, u + 1)
                    if u:
                        pe.wait_ge(eva, u)
                        if sum(wide[:u]):
                            pe.wait_ge(evb, sum(wide[:u]))
                    for c in range(keys[u] // P):
                        mm = nc.tensor.transpose(tr[:, c // 4, (c % 4) * P:(c % 4 + 1) * P], E[:, u % 2, 0, c * P:(c + 1) * P], m.ident)
                    mm.then_inc(trs, 1)
                    if u:
                        output(u - 1)
                output(N - 1)

            @block.scalar
            def _(act):
                for t in range(NT):
                    act.wait_ge(prep, t + 1)
                    if t < tq:
                        act.nop().then_inc(evq, 1)
                        continue
                    for half in range(2):
                        rows = slice(64 * half, 64 * half + 64)
                        ins = nc.scalar.activation(QT[rows, :, half, t * P:(t + 1) * P],
                                                   S[rows, t % 2, 0:CQ * P].rearrange("p (c n) -> p c n", n=P),
                                                   ACT.Copy, scale=64 ** -0.5)
                    ins.then_inc(evq, 1)
                if diff:
                    act.wait_ge(lams, 1)
                    nc.scalar.activation(lamv[:, 2:4], lamv[:, 0:2], ACT.Exp).then_inc(lexp, 1)

                def exponentials(u):
                    t, h = units[u]
                    s, r, nk = u % 2, u % 3, keys[u]
                    if u >= 2:
                        act.wait_ge(trs, u - 1)
                    for j in range(maps):
                        g = maps * u + j
                        act.wait_ge(negs, g + 1)
                        neg = stat[:, r, j:j + 1]
                        if diff or not wide[u]:
                            nc.scalar.activation(E[:, s, j, 0:nk], S[:, g % 2, 0:nk], ACT.Exp, bias=neg,
                                                 accum_out=stat[:, r, 4 + j:5 + j]).then_inc(exps, 1)
                        else:
                            nc.scalar.activation(E[:, s, 0, 0:CTX], S[:, g % 2, 0:CTX], ACT.Exp, bias=neg,
                                                 accum_out=stat[:, r, 4:5])
                            nc.scalar.activation(E[:, s, 0, CTX:TOK], SB[:, s], ACT.Exp, bias=neg,
                                                 accum_out=stat[:, r, 5:6]).then_inc(exps, 1)

                def final(u):
                    t, h = units[u]
                    act.wait_ge(outs, u + 1)
                    factor = stat[:, u % 3, 8:9]
                    nc.scalar.activation(Y[:, t, y0 + h * dv:y0 + (h + 1) * dv], O[:, u % 2, 0:dv], ACT.Copy, scale=factor)
                    if u:
                        act.wait_ge(oev, u)
                    nc.scalar.activation(sq[:, 0:dv], O[:, u % 2, 0:dv], ACT.Square, scale=factor,
                                         accum_out=rstat[:, 0, u:u + 1]).then_inc(oev, 1)

                exponentials(0)
                for u in range(N):
                    if u + 1 < N:
                        exponentials(u + 1)
                    act.wait_ge(trs, u + 1)
                    if u >= 2:
                        act.wait_ge(outs, u - 1)
                    n = min(keys[u], 512)
                    nc.scalar.activation(AT[:, u % 2, 0:n], tr[:, 0, 0:n], ACT.Copy).then_inc(eva, 1)
                    if diff and u >= 2:
                        final(u - 2)
                    if not diff and u == SILU_AT:
                        nc.scalar.activation(g_silu[:, tq:NT], PR[:, tq:NT, GR:GR + 256], ACT.Silu).then_inc(g_silus, 1)
                    if not diff and u == ROOT_AT:
                        act.wait_ge(g_mean, 1)
                        nc.scalar.activation(g_stat[:, 2, 0:n_out * HEADS], g_stat[:, 1, 0:n_out * HEADS], ACT.Sqrt).then_inc(g_root, 1)
                if diff:
                    final(N - 2)
                    final(N - 1)

            @block.vector
            def _(dve):
                link = linker(dve, chain)
                nc.vector.memset(QT[64:128, :, 0], 0.0).then_inc(zeroed, 1)
                nc.vector.memset(QT[0:64, :, 1], 0.0).then_inc(zeroed, 1)
                for t in range(NT):
                    dve.wait_ge(prep, t + 1)
                    nc.vector.tensor_copy(KT[:, :, t * P:(t + 1) * P], S[:, t % 2, 512:512 + CQ * P].rearrange(
                        "p (c n) -> p c n", n=P)).then_inc(evk, 1)
                if diff:
                    dve.wait_ge(loads, 16)
                    nc.vector.tensor_tensor_reduce(out=sq[:, 0:64], in0=lam[:, 0], in1=lam[:, 1], scale=1.0, scalar=0.0,
                                                   op0=ALU.mult, op1=ALU.add, accum_out=lamv[:, 0:1])
                    nc.vector.tensor_tensor_reduce(out=sq[:, 64:128], in0=lam[:, 2], in1=lam[:, 3], scale=1.0, scalar=0.0,
                                                   op0=ALU.mult, op1=ALU.add, accum_out=lamv[:, 1:2]).then_inc(lams, 1)
                    dve.wait_ge(lexp, 1)
                    link(nc.vector.tensor_tensor(lamv[:, 4:5], lamv[:, 3:4], lamv[:, 2:3], ALU.subtract))
                    link(nc.vector.tensor_scalar(lamv[:, 5:6], lamv[:, 4:5], lam_init(l), None, ALU.subtract))

                def maxima(u):
                    t, h = units[u]
                    s, r, nk = u % 2, u % 3, keys[u]
                    for j in range(maps):
                        g = maps * u + j
                        dve.wait_ge(scores, g + 1)
                        if diff or not wide[u]:
                            nc.vector.tensor_reduce(stat[:, r, j:j + 1], S[:, g % 2, 0:nk], AX_X, ALU.max, negate=True).then_inc(negs, 1)
                            continue
                        link(nc.vector.tensor_reduce(stat[:, r, 2:3], S[:, g % 2, 0:CTX], AX_X, ALU.max))
                        if u == first_wide:
                            dve.wait_ge(biased, HEADS)
                        first = 7 - 2 * (t - CT)
                        link(nc.vector.tensor_tensor_reduce(
                            out=SB[:, s], in0=S[:, g % 2, CTX:TOK], in1=bias[:, h, first:first + 8].rearrange("p r c -> p (r c)"),
                            scale=1.0, scalar=stat[:, r, 2:3], op0=ALU.add, op1=ALU.max, accum_out=stat[:, r, 3:4]))
                        nc.vector.tensor_scalar(stat[:, r, 0:1], stat[:, r, 3:4], -1.0, None, ALU.mult).then_inc(negs, 1)

                def combine(u):
                    s, r, nk = u % 2, u % 3, keys[u]
                    dve.wait_ge(exps, maps * (u + 1))
                    if u >= 3:
                        dve.wait_ge(oev, u - 2)
                    if diff:
                        link(nc.vector.reciprocal(stat[:, r, 8:10], stat[:, r, 4:6]))
                        link(nc.vector.scalar_tensor_tensor(out=stat[:, r, 10:11], in0=stat[:, r, 4:5], scalar=stat[:, r, 9:10],
                                                            in1=lamv[:, 5:6], op0=ALU.mult, op1=ALU.mult))
                        nc.vector.scalar_tensor_tensor(out=E[:, s, 0, 0:nk], in0=E[:, s, 1, 0:nk], scalar=stat[:, r, 10:11],
                                                       in1=E[:, s, 0, 0:nk], op0=ALU.mult, op1=ALU.add).then_inc(probs, 1)
                    elif wide[u]:
                        link(nc.vector.tensor_tensor(stat[:, r, 6:7], stat[:, r, 4:5], stat[:, r, 5:6], ALU.add))
                        link(nc.vector.reciprocal(stat[:, r, 8:9], stat[:, r, 6:7]))
                    else:
                        link(nc.vector.reciprocal(stat[:, r, 8:9], stat[:, r, 4:5]))

                def final(u):
                    t, h = units[u]
                    dve.wait_ge(outs, u + 1)
                    nc.vector.tensor_scalar(Y[:, t, y0 + h * dv:y0 + (h + 1) * dv], O[:, u % 2, 0:dv], stat[:, u % 3, 8:9],
                                            None, ALU.mult).then_inc(oev, 1)

                done = None if diff else linker(dve, g_chain)

                def gla_output(step):
                    o, n = Y[:, tq:NT, 0:256], n_out * HEADS
                    if step == 0:
                        done(nc.vector.tensor_tensor(g_sq[:, tq:NT], o, o, ALU.mult))
                    elif step == 1:
                        done(nc.vector.tensor_reduce(g_stat[:, 0, 0:n], g_sq[:, tq:NT].rearrange("p t (h v) -> p (t h) v", v=64),
                                                     AX_X, ALU.add))
                    elif step == 2:
                        nc.vector.tensor_scalar(g_stat[:, 1, 0:n], g_stat[:, 0, 0:n], 1.0 / 64, EPS, ALU.mult, ALU.add).then_inc(g_mean, 1)
                    elif step == 3:
                        dve.wait_ge(g_gains, 16)
                        done(nc.vector.tensor_tensor(o, o, bcast(g_gain[:], 1, n_out), ALU.mult))
                    elif step == 4:
                        dve.wait_ge(g_silus, 1)
                        done(nc.vector.tensor_tensor(o, o, g_silu[:, tq:NT], ALU.mult))
                    elif step == 5:
                        dve.wait_ge(g_root, 1)
                        done(nc.vector.reciprocal(g_stat[:, 3, 0:n], g_stat[:, 2, 0:n]))
                    else:
                        for i in range(n_out):
                            oh = Y[:, tq + i, 0:256].rearrange("p (h v) -> p h v", v=64)
                            nc.vector.tensor_tensor(oh, oh, stretch(g_stat[:, 3, i * HEADS:(i + 1) * HEADS].rearrange(
                                "p (h o) -> p h o", o=1), 64), ALU.mult)

                maxima(0)
                for u in range(N):
                    if diff:
                        combine(u)
                    if u + 1 < N:
                        maxima(u + 1)
                    if not diff:
                        combine(u)
                    if wide[u]:
                        dve.wait_ge(trs, u + 1)
                        if u >= 2:
                            dve.wait_ge(outs, u - 1)
                        nc.vector.tensor_copy(AT[:, u % 2, 512:TOK], tr[:, 1, 0:256]).then_inc(evb, 1)
                    if not diff and u >= 2:
                        final(u - 2)
                    if not diff and u in G_STEPS:
                        gla_output(u - G_STEPS[0])
                if not diff:
                    final(N - 2)
                    final(N - 1)


def out_project(nc, m, l, t0, Y):
    tiles = list(range(t0, NT))
    n = len(tiles) * HEADS
    rstat = m.rstat
    with Stage(nc, f"out{l}") as st:
        w = st.sb("w", [P, KD, D])
        gate = st.sb("gate", [P, 2, D])
        YT = st.sb("YT", [P, KD, TOK])
        part = st.sb("part", [P, 2, 512])
        tr = st.ps("tr", [P, 2, 2, 512])
        acc = st.ps("acc", [P, 4, 512])
        gain, junk = st.sb("gain", [P, 512]), st.sb("junk", [P, D])
        squared = st.sem("squared")
        gains, means, roots, chain, normed = (st.sem(x) for x in ("gains", "means", "roots", "chain", "normed"))
        ws, gates, trs, ev0, ev1, prods, scaled, added = (st.sem(x) for x in (
            "w", "gates", "trs", "ev0", "ev1", "prods", "scaled", "added"))
        with nc.Block() as block:
            @block.sync
            def _(sp):
                sp.dma_start(gain[:], row_bcast(m.a["diff_norm_g"][l])).then_inc(gains, 16)
                sp.dma_start(w[:], m.a["w_out"][l].rearrange("(k p) n -> p k n", p=P)).then_inc(ws, 16)
                for s in range(2):
                    sp.dma_start(gate[:, s], row_bcast(mod_row(m, l, 1 - s, 2))).then_inc(gates, 16)

            @block.tensor
            def _(pe):
                for i, t in enumerate(tiles):
                    if i >= 2:
                        pe.wait_ge(ev0, i - 1)
                        pe.wait_ge(ev1, i - 1)
                    for k in range(KD):
                        if k == KD // 2:
                            pe.wait_ge(normed, i + 1)
                        mm = nc.tensor.transpose(tr[:, i % 2, k // 4, (k % 4) * P:(k % 4 + 1) * P],
                                                 Y[:, t, k * P:(k + 1) * P], m.ident)
                    mm.then_inc(trs, 1)
                pe.wait_ge(ws, 16)
                for i, t in enumerate(tiles):
                    pe.wait_ge(ev0, i + 1)
                    pe.wait_ge(ev1, i + 1)
                    for half in range(2):
                        j = 2 * i + half
                        if j >= 4:
                            pe.wait_ge(scaled, j - 3)
                        for k in range(KD):
                            mm = nc.tensor.matmul(acc[:, j % 4], YT[:, k, t * P:(t + 1) * P], w[:, k, half * 512:(half + 1) * 512],
                                                  start=k == 0, stop=k == KD - 1)
                        mm.then_inc(prods, 1)

            @block.scalar
            def _(act):
                act.wait_ge(means, 1)
                nc.scalar.activation(rstat[:, 2, 0:n], rstat[:, 1, 0:n], ACT.Sqrt).then_inc(roots, 1)
                for i, t in enumerate(tiles):
                    act.wait_ge(trs, i + 1)
                    nc.scalar.activation(YT[:, 0:4, t * P:(t + 1) * P], tr[:, i % 2, 0].rearrange("p (k n) -> p k n", n=P),
                                         ACT.Copy).then_inc(ev0, 1)
                for i, t in enumerate(tiles):
                    act.wait_ge(added, 2 * i + 2)
                    if i:
                        act.wait_ge(squared, i)
                    nc.scalar.activation(junk[:], m.X[:, t], ACT.Square, accum_out=m.ssq[:, t:t + 1]).then_inc(squared, 1)

            @block.vector
            def _(dve):
                link = linker(dve, chain)
                nc.vector.tensor_scalar(rstat[:, 1, 0:n], rstat[:, 0, 0:n], 1.0 / 128, EPS, ALU.mult, ALU.add).then_inc(means, 1)
                dve.wait_ge(gains, 16)
                link(nc.vector.tensor_scalar(gain[:], gain[:], 1.0 - lam_init(l), None, ALU.mult))
                dve.wait_ge(roots, 1)
                link(nc.vector.reciprocal(rstat[:, 3, 0:n], rstat[:, 2, 0:n]))

                def evacuate(i):
                    t = tiles[i]
                    dve.wait_ge(trs, i + 1)
                    nc.vector.tensor_copy(YT[:, 4:8, t * P:(t + 1) * P],
                                          tr[:, i % 2, 1].rearrange("p (k n) -> p k n", n=P)).then_inc(ev1, 1)

                for i, t in enumerate(tiles):
                    for h in range(HEADS):
                        o = Y[:, t, 512 + h * 128:640 + h * 128]
                        ins = nc.vector.scalar_tensor_tensor(out=o, in0=o, scalar=rstat[:, 3, i * HEADS + h:i * HEADS + h + 1],
                                                             in1=gain[:, h * 128:(h + 1) * 128], op0=ALU.mult, op1=ALU.mult)
                    ins.then_inc(normed, 1)
                    if i:
                        evacuate(i - 1)
                evacuate(len(tiles) - 1)
                dve.wait_ge(gates, 32)
                for i, t in enumerate(tiles):
                    for half in range(2):
                        j = 2 * i + half
                        dve.wait_ge(prods, j + 1)
                        if j >= 2:
                            dve.wait_ge(added, j - 1)
                        nc.vector.tensor_tensor(part[:, j % 2], acc[:, j % 4], gate[:, 0 if t < CT else 1, half * 512:(half + 1) * 512],
                                                ALU.mult).then_inc(scaled, 1)

            @block.gpsimd
            def _(pool):
                for i, t in enumerate(tiles):
                    for half in range(2):
                        j = 2 * i + half
                        x = m.X[:, t, half * 512:(half + 1) * 512]
                        pool.wait_ge(scaled, j + 1)
                        nc.gpsimd.tensor_tensor(x, x, part[:, j % 2], ALU.add).then_inc(added, 1)


def finish(nc, m, out):
    with Stage(nc, "finish") as st:
        g, junk, stat, y = st.sb("g", [P, D]), st.sb("junk", [P, D]), st.sb("stat", [P, 4, LT]), st.sb("y", [P, LT, D])
        rows, ssq, mean, root, inv, ys, stored = (st.sem(x) for x in ("rows", "ssq", "mean", "root", "inv", "y", "stored"))
        with nc.Block() as block:
            @block.sync
            def _(sp):
                sp.dma_start(g[:], row_bcast(m.a["final_g"])).then_inc(rows, 16)
                for t in range(LT):
                    sp.wait_ge(ys, t + 1)
                    sp.dma_start(out[0, t * P:(t + 1) * P], y[:, t]).then_inc(stored, 16)
                sp.wait_ge(stored, 16 * LT)

            @block.scalar
            def _(act):
                for t in range(LT):
                    if t:
                        act.wait_ge(ssq, t)
                    nc.scalar.activation(junk[:], m.X[:, CT + t], ACT.Square, accum_out=stat[:, 0, t:t + 1]).then_inc(ssq, 1)
                act.wait_ge(mean, 1)
                nc.scalar.activation(stat[:, 2], stat[:, 1], ACT.Sqrt).then_inc(root, 1)

            @block.vector
            def _(dve):
                dve.wait_ge(ssq, LT)
                nc.vector.tensor_scalar(stat[:, 1], stat[:, 0], 1.0 / D, EPS, ALU.mult, ALU.add).then_inc(mean, 1)
                dve.wait_ge(root, 1)
                nc.vector.reciprocal(stat[:, 3], stat[:, 2]).then_inc(inv, 1)
                dve.wait_ge(inv, 1)
                dve.wait_ge(rows, 16)
                for t in range(LT):
                    nc.vector.scalar_tensor_tensor(out=y[:, t], in0=m.X[:, CT + t], scalar=stat[:, 3, t:t + 1], in1=g[:],
                                                   op0=ALU.mult, op1=ALU.mult).then_inc(ys, 1)


def peer(nc, m, l, t0):
    with ExitStack() as ctx:
        def sb(name, shape, dt=F32):
            return ctx.enter_context(nc.sbuf_tensor(f"peer{l}_{name}", shape, dt))
        H = sb("H", [P, NT, D])
        QT = sb("QT", [P, PH, (NT + 1) * P])
        sub = sb("sub", [P, NKEYS])
        s = Model()
        s.QT, s.sub, s.H = QT, sub, H
        s.val, s.idx = sb("val", [P, 2, PH, TOPK]), sb("idx", [P, 2, PH, TOPK], U32)
        s.top, s.pos = sb("top", [P, PH, TOPK]), sb("pos", [P, PH, TOPK], U32)
        s.rest, s.cand = sb("rest", [P, 2, NKEYS]), sb("cand", [P, 256])
        s.idxf, s.part, s.partf = sb("idxf", [P, 2, PH, TOPK]), sb("part", [P, 2, SLOTS], U32), sb("partf", [P, 2, SLOTS])
        s.hot, s.sel = sb("hot", [P, SLOTS, TOPK]), sb("sel", [P, 3, SLOTS])
        s.soft, s.sums = sb("soft", [P, SLOTS]), sb("sums", [P, 2, PH])
        s.expert, s.gate = sb("expert", [P, 2, SLOTS], U32), sb("gate", [P, 2, SLOTS])
        s.iota = m.iota
        with nc.sbuf_tensor(f"H2T{l}", [P, KD, TOK], F32) as HT:
            peer_queries(nc, m, l, t0, HT, s)
        s.h, s.q = sb("h", [P, 2, D]), sb("q", [P, PH, 2 * P])
        s.dots, s.gelu, s.w = sb("dots", [P, 2 * SLOTS]), sb("gelu", [P, 2 * SLOTS]), sb("w", [P, 2 * SLOTS])
        s.U, s.V = sb("U", [P, RING, D]), sb("V", [P, RING, D])
        s.diag = sb("diag", [P, 4, P])
        s.G, s.part_out = sb("G", [P, D]), sb("partout", [P, D])
        if l + 1 < DEPTH:
            s.ada, s.rows = sb("ada", [P, KD, 256]), sb("adarows", [2, 2 * 512])
        if t0 < CT:
            peer_tiles(nc, m, l, 0, CT, 1, s)
        peer_tiles(nc, m, l, CT, NT, 0, s)


def peer_queries(nc, m, l, t0, HT, s):
    spans = [(t0 * P, t0 * P + 256), (t0 * P + 256, TOK)]
    work = [(h, a, b) for a, b in spans for h in range(PH)]
    SEARCH_AT = [3, 7, 10, 12] if t0 == 0 else [3, 7, 11, 15]
    SOFT_AFTER = 13 if t0 == 0 else 15
    with Stage(nc, f"query{l}") as st:
        w = st.sb("w", [P, KD, D])
        rows = st.sb("rows", [NKEYS, 2, 64])
        scratch = st.sb("scratch", [P, 6, D])
        acc = st.ps("acc", [P, 2, 512])
        ps = st.ps("keys", [P, 2, 512])
        sems = search_sems(st)
        ws = [st.sem("w0"), st.sem("w1")]
        ht = st.sem("ht0"), st.sem("ht1")
        keys, trs, turned, prods = (st.sem(x) for x in ("keys", "trs", "turned", "prods"))
        with nc.Block() as block:
            norm_modulate(nc, m, l, m.a["norm2_g"][l], 3, t0, HT, st, block, ht, scratch, s.H, squares=False)

            @block.sync
            def _(sp):
                sp.dma_start(rows[:], m.a["peer_subkeys"][l].rearrange("s n d -> n s d")).then_inc(keys, 16)
                for i in range(2):
                    sp.dma_start(w[:, :, 512 * i:512 * i + 512], m.a["peer_wq"][l].rearrange("(k p) n -> p k n", p=P)[
                        :, :, 512 * i:512 * i + 512]).then_inc(ws[i], 16)

            @block.tensor
            def _(pe):
                pe.wait_ge(keys, 16)
                nc.tensor.transpose(ps[:, 0, 0:NKEYS], rows[:].rearrange("n s d -> n (s d)"), m.ident).then_inc(trs, 1)
                for i, (h, a, b) in enumerate(work):
                    if i in SEARCH_AT:
                        step = SEARCH_AT.index(i)
                        pe.wait_ge(turned, 1)
                        key_scores(nc, pe, s, sems, ps, step, s.QT[:, :, t0 * P:(t0 + 1) * P], 2 * step + 2)
                    pe.wait_ge(ws[h // 4], 16)
                    if i == 0 or work[i - 1][2] != b:
                        pe.wait_ge(ht[0], b // P - t0)
                        pe.wait_ge(ht[1], b // P - t0)
                    if i >= 2:
                        pe.wait_ge(sems.queries, i - 1)
                    for k in range(KD):
                        mm = nc.tensor.matmul(acc[:, i % 2, 0:b - a], w[:, k, h * P:(h + 1) * P], HT[:, k, a:b],
                                              start=k == 0, stop=k == KD - 1)
                    mm.then_inc(prods, 1)

            @block.scalar
            def _(act):
                for i, (h, a, b) in enumerate(work):
                    act.wait_ge(prods, i + 1)
                    nc.scalar.activation(s.QT[:, h, a:b], acc[:, i % 2, 0:b - a], ACT.Copy).then_inc(sems.queries, 1)
                    if i == SOFT_AFTER:
                        softmax_exp(nc, act, s, sems, 0)

            @block.vector
            def _(dve):
                link = linker(dve, sems.chain)
                nc.vector.memset(s.QT[:, :, TOK:TOK + P], 0.0)
                dve.wait_ge(trs, 1)
                nc.vector.tensor_copy(s.sub[:], ps[:, 0, 0:NKEYS]).then_inc(turned, 1)
                for h in range(PH):
                    search(nc, dve, link, s, sems, ps, h)
                select(nc, dve, link, s, sems, l, 0, 0)


def key_scores(nc, pe, s, sems, ps, step, queries, ready):
    pe.wait_ge(sems.queries, ready)
    if step:
        pe.wait_ge(sems.searched, 2 * step)
    for n in range(2 * step, 2 * step + 2):
        j, h = divmod(n, PH)
        for half in range(2):
            rows = slice(64 * half, 64 * half + 64)
            mm = nc.tensor.matmul(ps[:, half, n % 2 * NKEYS:(n % 2 + 1) * NKEYS], queries[rows, h, j * P:(j + 1) * P],
                                  s.sub[rows], start=True, stop=True)
    mm.then_inc(sems.keyed, 1)


def search(nc, dve, link, s, sems, ps, n):
    h = n % PH
    dve.wait_ge(sems.keyed, n // 2 + 1)
    cols = slice(n % 2 * NKEYS, (n % 2 + 1) * NKEYS)
    val, idx = s.val[:, :, h], s.idx[:, :, h]
    for half in range(2):
        ins = nc.vector.max(val[:, half, 0:8], ps[:, half, cols])
    link(ins)
    for half in range(2):
        nc.vector.max_index(idx[:, half, 0:8], val[:, half, 0:8], ps[:, half, cols])
        ins = nc.vector.match_replace(s.rest[:, half], val[:, half, 0:8], ps[:, half, cols], NEG)
    ins.then_inc(sems.searched, 1)
    dve.wait_ge(sems.searched, n + 1)
    for half in range(2):
        ins = nc.vector.max(val[:, half, 8:16], s.rest[:, half])
    link(ins)
    for half in range(2):
        nc.vector.max_index(idx[:, half, 8:16], val[:, half, 8:16], s.rest[:, half])
    cand = s.cand[:].rearrange("p (i j) -> p i j", j=TOPK)
    link(nc.vector.tensor_tensor(cand, stretch(val[:, 0].rearrange("p (i o) -> p i o", o=1), TOPK), bcast(val[:, 1], 1, TOPK), ALU.add))
    top, pos, rest = s.top[:, h], s.pos[:, h], s.rest[:].rearrange("p a b -> p (a b)")
    link(nc.vector.max(top[:, 0:8], s.cand[:]))
    nc.vector.max_index(pos[:, 0:8], top[:, 0:8], s.cand[:])
    link(nc.vector.match_replace(rest, top[:, 0:8], s.cand[:], NEG))
    link(nc.vector.max(top[:, 8:16], rest))
    link(nc.vector.max_index(pos[:, 8:16], top[:, 8:16], rest))


def select(nc, dve, link, s, sems, l, j, place):
    largest = s.top[:, :, 0:1]
    nc.vector.tensor_tensor(s.soft[:].rearrange("p (h k) -> p h k", k=TOPK), s.top[:], stretch(largest, TOPK),
                            ALU.subtract).then_inc(sems.shifted, 1)
    pos = s.pos[:].rearrange("p h k -> p (h k)")
    nc.vector.tensor_scalar(s.part[:, 0], pos, 4, None, ALU.logical_shift_right)
    nc.vector.tensor_scalar(s.part[:, 1], pos, 15, None, ALU.bitwise_and)
    link(nc.vector.tensor_copy(s.idxf[:], s.idx[:]))
    link(nc.vector.tensor_copy(s.partf[:], s.part[:]))
    for half in range(2):
        link(nc.vector.tensor_tensor(s.hot[:], stretch(s.partf[:, half].rearrange("p (n o) -> p n o", o=1), TOPK),
                                     bcast(s.iota, 1, SLOTS), ALU.is_equal))
        hot = s.hot[:].rearrange("p (h k) j -> p h k j", h=PH)
        link(nc.vector.tensor_tensor(hot, hot, bcast(s.idxf[:, half], 2, TOPK), ALU.mult))
        link(nc.vector.tensor_reduce(s.sel[:, half], s.hot[:], AX_X, ALU.add))
    link(nc.vector.scalar_tensor_tensor(out=s.sel[:, 2], in0=s.sel[:, 0], scalar=float(NKEYS), in1=s.sel[:, 1],
                                        op0=ALU.mult, op1=ALU.add))
    dve.wait_ge(sems.soft, j + 1)
    soft = s.soft[:].rearrange("p (h k) -> p h k", k=TOPK)
    link(nc.vector.tensor_reduce(s.sums[:, 0], soft, AX_X, ALU.add))
    link(nc.vector.reciprocal(s.sums[:, 1], s.sums[:, 0]))
    link(nc.vector.tensor_tensor(s.gate[:, place].rearrange("p (h k) -> p h k", k=TOPK), soft,
                                 stretch(s.sums[:, 1].rearrange("p (h o) -> p h o", o=1), TOPK), ALU.mult))
    nc.vector.tensor_scalar(s.expert[:, place], s.sel[:, 2], float(l * EXPERTS), None, ALU.add).then_inc(sems.chosen, 1)
    dve.wait_ge(sems.chosen, j + 1)


def softmax_exp(nc, act, s, sems, j):
    act.wait_ge(sems.shifted, j + 1)
    nc.scalar.activation(s.soft[:], s.soft[:], ACT.Exp).then_inc(sems.soft, 1)


def search_sems(st):
    sems = Model()
    sems.queries, sems.keyed, sems.searched, sems.shifted, sems.soft, sems.chosen, sems.chain = (
        st.sem(x) for x in ("queries", "keyed", "searched", "shifted", "soft", "chosen", "chain"))
    return sems


def peer_tiles(nc, m, l, first, end, stream, s):
    with Stage(nc, f"gate{l}_{stream}") as st:
        gates = st.sem("gates")
        with nc.Block() as block:
            @block.sync
            def _(sp):
                sp.dma_start(s.G[:], row_bcast(mod_row(m, l, stream, 5))).then_inc(gates, 16)
                sp.wait_ge(gates, 16)
    u_rows, v_rows = (m.a[n].rearrange("l e d -> (l e) d") for n in ("peer_u", "peer_v"))
    more = l + 1 < DEPTH
    CHUNKS, CW = 8, 256
    MOD_AT, MOD_ADD = [2, 3, 4, 5, 9, 10, 11, 12], [6, 13]
    with nc.Fori(first // 2, end // 2) as pair:
        t = pair * 2
        with Stage(nc, f"tile{l}_{stream}") as st:
            acc = st.ps("acc", [P, 2, 2, 512])
            ps = st.ps("keys", [P, 2, 512])
            mod = st.ps("mod", [P, 2, 512])
            sems = search_sems(st)
            ug, vg = m.ug, m.vg
            st.gathers = ug + vg
            h_now, dots, gelus, weights, diags, sums, scaled = (st.sem(x) for x in (
                "hnow", "dots", "gelus", "weights", "diags", "vsums", "scaled"))
            adas, rows_in, modded, added, stored = (st.sem(x) for x in ("adas", "rowsin", "modded", "added", "stored"))
            NH = 2 * PH
            STEPS = {h: h % PH + h // PH * (PH // 2) for h in range(NH) if h % PH < PH // 2}
            with nc.Block() as block:
                @block.gpsimd
                def _(pool):
                    for h in range(NH + 1):
                        if h == PH:
                            pool.wait_ge(sems.chosen, 1)
                        for k in range(TOPK):
                            if h < NH:
                                n = h * TOPK + k
                                if n >= RING:
                                    pool.wait_ge(dots, n - RING + 1)
                                pool.indirect_dma_start(s.U[:, n % RING], None, u_rows, bass.IndirectOffsetOnAxis(
                                    ap=s.expert[:, n // SLOTS, n % SLOTS:n % SLOTS + 1], axis=0)).then_inc(ug[n % RING], 16)
                            if h:
                                n = (h - 1) * TOPK + k
                                if n >= RING:
                                    pool.wait_ge(sums, n - RING + 1)
                                pool.indirect_dma_start(s.V[:, n % RING], None, v_rows, bass.IndirectOffsetOnAxis(
                                    ap=s.expert[:, n // SLOTS, n % SLOTS:n % SLOTS + 1], axis=0)).then_inc(vg[n % RING], 16)
                    for done in ug + vg:
                        pool.wait_ge(done, 16 * (2 * SLOTS // RING))

                if more:
                    @block.sync
                    def _(sp):
                        w, b = m.ada_w[l + 1].rearrange("(k p) n -> p k n", p=P), m.ada_b[l + 1:l + 2]
                        for i in range(CHUNKS):
                            if i:
                                sp.wait_ge(modded, i)
                            sp.dma_start(s.ada[:], w[:, :, bass.ds(t * (CHUNKS * CW // 2) + i * CW, CW)]).then_inc(adas, 16)
                            if i % 4 == 0:
                                if i:
                                    sp.wait_ge(stored, 16 * (i // 4))
                                for row in range(2):
                                    sp.dma_start(s.rows[row:row + 1], b[:, bass.ds(t * (CHUNKS * CW // 2) + i * CW, 4 * CW)]).then_inc(rows_in, 16)
                            if i % 4 == 3:
                                sp.wait_ge(added, i // 4 + 1)
                                sp.dma_start(m.mods[l + 1][:, bass.ds(t * (CHUNKS * CW // 2) + (i - 3) * CW, 4 * CW)],
                                             s.rows[:]).then_inc(stored, 16)
                        sp.wait_ge(stored, 16 * (CHUNKS // 4))

                @block.scalar
                def _(act):
                    nc.scalar.activation(s.h[:], s.H[:, bass.ds(t, 2), :], ACT.Copy).then_inc(h_now, 1)
                    nc.scalar.activation(s.q[:], s.QT[:, :, bass.ds((t + 1) * P, 2 * P)], ACT.Copy).then_inc(sems.queries, 1)
                    for h in range(NH + 1):
                        if h % PH == PH // 2 + 1:
                            softmax_exp(nc, act, s, sems, h // PH)
                        if h:
                            act.wait_ge(weights, h)
                            for n in range((h - 1) * TOPK, h * TOPK):
                                if n >= 4:
                                    act.wait_ge(sums, n - 3)
                                nc.scalar.activation(s.diag[:, n % 4], m.ident, ACT.Copy, scale=s.w[:, n:n + 1]).then_inc(diags, 1)
                        if h < NH:
                            act.wait_ge(dots, TOPK * (h + 1))
                            nc.scalar.activation(s.gelu[:, h * TOPK:(h + 1) * TOPK], s.dots[:, h * TOPK:(h + 1) * TOPK],
                                                 ACT.Gelu_apprx_tanh).then_inc(gelus, 1)

                @block.tensor
                def _(pe):
                    for h in range(NH + 1):
                        if h in STEPS:
                            key_scores(nc, pe, s, sems, ps, STEPS[h], s.q, 1)
                        if more and h in MOD_AT:
                            i = MOD_AT.index(h)
                            pe.wait_ge(adas, 16 * (i + 1))
                            if i >= 4 and i % 2 == 0:
                                pe.wait_ge(added, 1)
                            for k in range(KD):
                                mm = nc.tensor.matmul(mod[0:2, i // 2 % 2, i % 2 * CW:i % 2 * CW + CW], m.silu[:, :, k], s.ada[:, k],
                                                      start=k == 0, stop=k == KD - 1)
                            mm.then_inc(modded, 1)
                        if h:
                            for n in range((h - 1) * TOPK, h * TOPK):
                                pe.wait_ge(diags, n + 1)
                                pe.wait_ge(vg[n % RING], 16 * (n // RING + 1))
                                for half in range(2):
                                    mm = nc.tensor.matmul(acc[:, n // SLOTS, half], s.diag[:, n % 4],
                                                          s.V[:, n % RING, 512 * half:512 * half + 512],
                                                          start=n % SLOTS == 0, stop=n % SLOTS == SLOTS - 1)
                                mm.then_inc(sums, 1)

                @block.vector
                def _(dve):
                    link = linker(dve, sems.chain)

                    def add_out(j):
                        dve.wait_ge(sums, SLOTS * (j + 1))
                        link(nc.vector.tensor_tensor(s.part_out[:], acc[:, j].rearrange("p a b -> p (a b)"), s.G[:], ALU.mult))
                        x = m.X[:, bass.ds(t + j, 1), :]
                        link(nc.vector.tensor_tensor(x, x, s.part_out[:].rearrange("p (o d) -> p o d", o=1), ALU.add))

                    dve.wait_ge(h_now, 1)
                    for h in range(NH):
                        for k in range(TOPK):
                            n = h * TOPK + k
                            dve.wait_ge(ug[n % RING], 16 * (n // RING + 1))
                            nc.vector.tensor_tensor_reduce(out=s.U[:, n % RING], in0=s.U[:, n % RING], in1=s.h[:, n // SLOTS],
                                                           scale=1.0, scalar=0.0, op0=ALU.mult, op1=ALU.add,
                                                           accum_out=s.dots[:, n:n + 1]).then_inc(dots, 1)
                        if h in STEPS:
                            search(nc, dve, link, s, sems, ps, 2 * STEPS[h])
                        cols = slice(h * TOPK, (h + 1) * TOPK)
                        gate = s.gate[:, h // PH, (h % PH) * TOPK:(h % PH + 1) * TOPK]
                        dve.wait_ge(gelus, h + 1)
                        nc.vector.tensor_tensor(s.w[:, cols], gate, s.gelu[:, cols], ALU.mult).then_inc(weights, 1)
                        if h in STEPS:
                            search(nc, dve, link, s, sems, ps, 2 * STEPS[h] + 1)
                        if h % PH == PH // 2:
                            select(nc, dve, link, s, sems, l, h // PH, 1 - h // PH)
                        if h == PH + 1:
                            add_out(0)
                        if more and h in MOD_ADD:
                            i = MOD_ADD.index(h)
                            dve.wait_ge(modded, 4 * (i + 1))
                            dve.wait_ge(rows_in, 32 * (i + 1))
                            nc.vector.tensor_tensor(s.rows[:], s.rows[:], mod[0:2].rearrange("p a b -> p (a b)"), ALU.add).then_inc(added, 1)
                    add_out(1)


def kernel(**inputs):
    import numpy as _np
    import concourse.bacc as _bacc
    from concourse import mybir as _mybir
    from concourse.bass_utils import run_bass_kernel_spmd as _run

    nc = _bacc.Bacc("TRN2", target_bir_lowering=False, num_devices=1)
    arrays, args = {}, {}
    for name, a in list(inputs.items()) + list(shape_constants().items()):
        a = _np.ascontiguousarray(a)
        arrays[f"in_{name}_dram"] = a
        args[name] = nc.dram_tensor(f"in_{name}_dram", a.shape, _mybir.dt.from_np(a.dtype), kind="ExternalInput").ap()
    out = nc.dram_tensor("out_dram", (1, SEQ, D), F32, kind="ExternalOutput").ap()
    build(nc, args, out)
    r = _run(nc, [arrays], core_ids=[0])
    return r.results[0]["out_dram"]
```
